# Optimizing a Trainium2 kernel written in Bass

```python
import jax, jax.numpy as jnp
from jax import lax
import numpy as np

D_MODEL = 1024
BATCH = 1
SEQ = 1024
DEPTH = 2
DEC_BATCH = 1
DEC_SEQ = 64
PAST_LEN = 1024

CHUNK = 64
Q_BLOCK = 128
FOX_HEADS = 8
FOX_HD = 64
FOX_W = FOX_HEADS * FOX_HD
FOX_SCALE = FOX_HD ** -0.5
SWA_HEADS = 8
SWA_KV_HEADS = 2
SWA_GROUP = SWA_HEADS // SWA_KV_HEADS
SWA_HD = 64
SWA_W = SWA_HEADS * SWA_HD
SWA_KV_W = SWA_KV_HEADS * SWA_HD
SWA_SCALE = SWA_HD ** -0.5
SWA_WINDOW = 128
SWA_BACK_CHUNKS = SWA_WINDOW // CHUNK
SWA_KEEP = SWA_WINDOW
MIX_W = FOX_W + SWA_W
IN_SPLITS = (FOX_W, 2 * FOX_W, 3 * FOX_W, 3 * FOX_W + FOX_HEADS, 3 * FOX_W + FOX_HEADS + SWA_W, 3 * FOX_W + FOX_HEADS + SWA_W + SWA_KV_W)
IN_COLS = 3 * FOX_W + FOX_HEADS + SWA_W + 2 * SWA_KV_W
N_MEM = 256
MEM_HEADS = 4
MEM_HD = 128
MEM_W = MEM_HEADS * MEM_HD
MEM_SCALE = MEM_HD ** -0.5
D_FF = 2816
CONV_W = 3
ROPE_THETA = 10000.0
EPS = 1e-6
NEG = -1e30

kernel_name = 'hymba_fox_swa_sink_convglu_stream_step'

def rms_norm(x, g):
    xf = x.astype(jnp.float32)
    y = xf * lax.rsqrt(jnp.mean(xf * xf, axis=-1, keepdims=True) + EPS)
    return (y * g.astype(jnp.float32)).astype(x.dtype)

def rope(x, pos):
    half = x.shape[-1] // 2
    inv_freq = ROPE_THETA ** (-jnp.arange(half, dtype=jnp.float32) / half)
    ang = pos.astype(jnp.float32)[:, None] * inv_freq[None, :]
    cos = jnp.cos(ang)[None, :, None, :]
    sin = jnp.sin(ang)[None, :, None, :]
    xf = x.astype(jnp.float32)
    x1, x2 = xf[..., :half], xf[..., half:]
    return jnp.concatenate([x1 * cos - x2 * sin, x1 * sin + x2 * cos], axis=-1).astype(x.dtype)

def project_heads(h, w_in, b_f):
    B, S, _ = h.shape
    qa, ka, va, fa, qb, kb, vb = jnp.split(h @ w_in, IN_SPLITS, axis=-1)
    logf = jax.nn.log_sigmoid(fa.astype(jnp.float32) + b_f.astype(jnp.float32))
    return (qa.reshape(B, S, FOX_HEADS, FOX_HD), ka.reshape(B, S, FOX_HEADS, FOX_HD),
            va.reshape(B, S, FOX_HEADS, FOX_HD), logf,
            qb.reshape(B, S, SWA_HEADS, SWA_HD), kb.reshape(B, S, SWA_KV_HEADS, SWA_HD),
            vb.reshape(B, S, SWA_KV_HEADS, SWA_HD))

def fox_attend(q, k, v, cq, ck, qpos, kpos):
    s = jnp.einsum('bqhd,bkhd->bhqk', q, k).astype(jnp.float32) * FOX_SCALE
    decay = jnp.swapaxes(cq, 1, 2)[:, :, :, None] - jnp.swapaxes(ck, 1, 2)[:, :, None, :]
    causal = kpos[None, :] <= qpos[:, None]
    p = jax.nn.softmax(jnp.where(causal, s + decay, NEG), axis=-1)
    return jnp.einsum('bhqk,bkhd->bqhd', p.astype(v.dtype), v)

def fox_prompt(q, k, v, logf):
    B, S, H, D = q.shape
    nb = S // Q_BLOCK
    c = jnp.cumsum(logf, axis=1)
    qb = jnp.moveaxis(q.reshape(B, nb, Q_BLOCK, H, D), 1, 0)
    cb = jnp.moveaxis(c.reshape(B, nb, Q_BLOCK, H), 1, 0)
    kpos = jnp.arange(S)

    def block(args):
        i, qi, ci = args
        return fox_attend(qi, k, v, ci, c, i * Q_BLOCK + jnp.arange(Q_BLOCK), kpos)

    o = lax.map(block, (jnp.arange(nb), qb, cb))
    return jnp.moveaxis(o, 0, 1).reshape(B, S, H * D)

def swa_attend(q, k, v, valid, sinks):
    s = jnp.einsum('bnqhgd,bnlhd->bnhgql', q, k).astype(jnp.float32) * SWA_SCALE
    s = jnp.where(valid[None, :, None, None, :, :], s, NEG)
    sink = sinks.astype(jnp.float32).reshape(1, 1, SWA_KV_HEADS, SWA_GROUP, 1, 1)
    m = jnp.maximum(jnp.max(s, axis=-1, keepdims=True), sink)
    e = jnp.exp(s - m)
    p = e / (jnp.sum(e, axis=-1, keepdims=True) + jnp.exp(sink - m))
    return jnp.einsum('bnhgql,bnlhd->bnqhgd', p.astype(v.dtype), v)

def swa_prompt(q, k, v, sinks):
    B, S = q.shape[:2]
    n = S // CHUNK
    qc = q.reshape(B, n, CHUNK, SWA_KV_HEADS, SWA_GROUP, SWA_HD)
    kc = k.reshape(B, n, CHUNK, SWA_KV_HEADS, SWA_HD)
    vc = v.reshape(B, n, CHUNK, SWA_KV_HEADS, SWA_HD)
    pad = jnp.zeros((B, SWA_BACK_CHUNKS, CHUNK, SWA_KV_HEADS, SWA_HD), k.dtype)
    kp = jnp.concatenate([pad, kc], axis=1)
    vp = jnp.concatenate([pad.astype(v.dtype), vc], axis=1)
    kband = jnp.concatenate([kp[:, j:j + n] for j in range(SWA_BACK_CHUNKS + 1)], axis=2)
    vband = jnp.concatenate([vp[:, j:j + n] for j in range(SWA_BACK_CHUNKS + 1)], axis=2)
    L = (SWA_BACK_CHUNKS + 1) * CHUNK
    key_chunk = jnp.arange(n)[:, None] - SWA_BACK_CHUNKS + (jnp.arange(L) // CHUNK)[None, :]
    valid = (key_chunk >= 0)[:, None, :]
    o = swa_attend(qc, kband, vband, valid, sinks)
    return o.reshape(B, S, SWA_W)

def memory_kv(mem, g, w_k, w_v):
    B, M, _ = mem.shape
    m = rms_norm(mem, g)
    return (m @ w_k).reshape(B, M, MEM_HEADS, MEM_HD), (m @ w_v).reshape(B, M, MEM_HEADS, MEM_HD)

def cross_attend(h, w_q, mk, mv, w_o):
    B, S, _ = h.shape
    q = (h @ w_q).reshape(B, S, MEM_HEADS, MEM_HD)
    s = jnp.einsum('bshd,bmhd->bhsm', q, mk).astype(jnp.float32) * MEM_SCALE
    p = jax.nn.softmax(s, axis=-1)
    o = jnp.einsum('bhsm,bmhd->bshd', p.astype(mv.dtype), mv)
    return o.reshape(B, S, MEM_W) @ w_o

def conv_ffn(h, w_up, w_conv, b_conv, w_down, state):
    S = h.shape[1]
    gate, val = jnp.split(h @ w_up, 2, axis=-1)
    gp = jnp.concatenate([state.astype(gate.dtype), gate], axis=1)
    conv = b_conv
    for j in range(CONV_W):
        conv = conv + w_conv[j] * gp[:, j:j + S]
    out = (jax.nn.silu(conv) * val) @ w_down
    return out, gp[:, -(CONV_W - 1):]

def setup_inputs(seed: int = 0) -> dict:
    key = jax.random.key(seed)
    k = jax.random.split(key, 32)

    def nrm(i, shape, scale):
        return scale * jax.random.normal(k[i], shape, jnp.float32)

    return {
        'x_prompt': nrm(0, (BATCH, SEQ, D_MODEL), 1.0),
        'x_sample': nrm(1, (DEC_BATCH, DEC_SEQ, D_MODEL), 1.0),
        'mem_prompt': nrm(2, (BATCH, N_MEM, D_MODEL), 1.0),
        'cache_fox_k': nrm(3, (DEPTH, DEC_BATCH, PAST_LEN, FOX_HEADS, FOX_HD), 1.0),
        'cache_fox_v': nrm(4, (DEPTH, DEC_BATCH, PAST_LEN, FOX_HEADS, FOX_HD), 1.0),
        'cache_fox_logf': jax.nn.log_sigmoid(3.0 + nrm(5, (DEPTH, DEC_BATCH, PAST_LEN, FOX_HEADS), 1.0)),
        'cache_swa_k': nrm(6, (DEPTH, DEC_BATCH, SWA_KEEP, SWA_KV_HEADS, SWA_HD), 1.0),
        'cache_swa_v': nrm(7, (DEPTH, DEC_BATCH, SWA_KEEP, SWA_KV_HEADS, SWA_HD), 1.0),
        'cache_mem_k': nrm(8, (DEPTH, DEC_BATCH, N_MEM, MEM_HEADS, MEM_HD), 1.0),
        'cache_mem_v': nrm(9, (DEPTH, DEC_BATCH, N_MEM, MEM_HEADS, MEM_HD), 1.0),
        'state_conv': nrm(10, (DEPTH, DEC_BATCH, CONV_W - 1, D_FF), 1.0),
        'ln_mix': 1.0 + nrm(11, (DEPTH, D_MODEL), 0.1),
        'w_in': nrm(12, (DEPTH, D_MODEL, IN_COLS), D_MODEL ** -0.5),
        'b_f': jax.random.uniform(k[13], (DEPTH, FOX_HEADS), jnp.float32, 1.0, 5.0),
        'swa_sinks': nrm(14, (DEPTH, SWA_HEADS), 0.5),
        'w_out': nrm(15, (DEPTH, MIX_W, D_MODEL), MIX_W ** -0.5),
        'ln_mem': 1.0 + nrm(16, (DEPTH, D_MODEL), 0.1),
        'ln_memtok': 1.0 + nrm(17, (DEPTH, D_MODEL), 0.1),
        'w_mq': nrm(18, (DEPTH, D_MODEL, MEM_W), D_MODEL ** -0.5),
        'w_mk': nrm(19, (DEPTH, D_MODEL, MEM_W), D_MODEL ** -0.5),
        'w_mv': nrm(20, (DEPTH, D_MODEL, MEM_W), D_MODEL ** -0.5),
        'w_mo': nrm(21, (DEPTH, MEM_W, D_MODEL), MEM_W ** -0.5),
        'ln_ffn': 1.0 + nrm(22, (DEPTH, D_MODEL), 0.1),
        'w_up': nrm(23, (DEPTH, D_MODEL, 2 * D_FF), D_MODEL ** -0.5),
        'w_conv': nrm(24, (DEPTH, CONV_W, D_FF), 0.5),
        'b_conv': nrm(25, (DEPTH, D_FF), 0.02),
        'w_down': nrm(26, (DEPTH, D_FF, D_MODEL), D_FF ** -0.5),
        'ln_final': 1.0 + nrm(27, (D_MODEL,), 0.1),
    }

def reference(x_prompt, x_sample, mem_prompt, cache_fox_k, cache_fox_v, cache_fox_logf,
              cache_swa_k, cache_swa_v, cache_mem_k, cache_mem_v, state_conv,
              ln_mix, w_in, b_f, swa_sinks, w_out, ln_mem, ln_memtok, w_mq, w_mk, w_mv, w_mo,
              ln_ffn, w_up, w_conv, b_conv, w_down, ln_final):
    B, S, _ = x_prompt.shape
    T = x_sample.shape[1]
    P = cache_fox_k.shape[2]
    pos_p = jnp.arange(S)
    pos_s = P + jnp.arange(T)
    xp, xs = x_prompt, x_sample
    fkp, fvp, flp, skp, svp, mkp, mvp, cvp = [], [], [], [], [], [], [], []
    fks, fvs, fls, sks, svs, cvs = [], [], [], [], [], []
    for l in range(DEPTH):
        h = rms_norm(xp, ln_mix[l])
        qa, ka, va, la, qb, kb, vb = project_heads(h, w_in[l], b_f[l])
        qb, kb = rope(qb, pos_p), rope(kb, pos_p)
        o = jnp.concatenate([fox_prompt(qa, ka, va, la), swa_prompt(qb, kb, vb, swa_sinks[l])], axis=-1)
        xp = xp + o @ w_out[l]
        fkp.append(ka); fvp.append(va); flp.append(la)
        skp.append(kb[:, -SWA_KEEP:]); svp.append(vb[:, -SWA_KEEP:])
        mk, mv = memory_kv(mem_prompt, ln_memtok[l], w_mk[l], w_mv[l])
        mkp.append(mk); mvp.append(mv)
        xp = xp + cross_attend(rms_norm(xp, ln_mem[l]), w_mq[l], mk, mv, w_mo[l])
        f, cst = conv_ffn(rms_norm(xp, ln_ffn[l]), w_up[l], w_conv[l], b_conv[l], w_down[l],
                          jnp.zeros((B, CONV_W - 1, D_FF), xp.dtype))
        xp = xp + f
        cvp.append(cst)
        h = rms_norm(xs, ln_mix[l])
        qa, ka, va, la, qb, kb, vb = project_heads(h, w_in[l], b_f[l])
        qb, kb = rope(qb, pos_s), rope(kb, pos_s)
        fk_all = jnp.concatenate([cache_fox_k[l].astype(ka.dtype), ka], axis=1)
        fv_all = jnp.concatenate([cache_fox_v[l].astype(va.dtype), va], axis=1)
        c_all = jnp.cumsum(jnp.concatenate([cache_fox_logf[l].astype(jnp.float32), la], axis=1), axis=1)
        oa = fox_attend(qa, fk_all, fv_all, c_all[:, P:], c_all, pos_s, jnp.arange(P + T))
        sk_all = jnp.concatenate([cache_swa_k[l].astype(kb.dtype), kb], axis=1)
        sv_all = jnp.concatenate([cache_swa_v[l].astype(vb.dtype), vb], axis=1)
        qc = qb.reshape(qb.shape[0], 1, T, SWA_KV_HEADS, SWA_GROUP, SWA_HD)
        valid = jnp.ones((1, 1, SWA_KEEP + T), dtype=bool)
        ob = swa_attend(qc, sk_all[:, None], sv_all[:, None], valid, swa_sinks[l])
        o = jnp.concatenate([oa.reshape(oa.shape[0], T, FOX_W), ob.reshape(ob.shape[0], T, SWA_W)], axis=-1)
        xs = xs + o @ w_out[l]
        fks.append(ka); fvs.append(va); fls.append(la)
        sks.append(sk_all[:, -SWA_KEEP:]); svs.append(sv_all[:, -SWA_KEEP:])
        xs = xs + cross_attend(rms_norm(xs, ln_mem[l]), w_mq[l], cache_mem_k[l].astype(xs.dtype),
                               cache_mem_v[l].astype(xs.dtype), w_mo[l])
        f, cst = conv_ffn(rms_norm(xs, ln_ffn[l]), w_up[l], w_conv[l], b_conv[l], w_down[l], state_conv[l])
        xs = xs + f
        cvs.append(cst)
    y_prompt = rms_norm(xp, ln_final)
    y_sample = rms_norm(xs, ln_final)
    st = lambda a: jnp.stack(a, axis=0)
    return (y_prompt, y_sample,
            st(fkp), st(fvp), st(flp), st(skp), st(svp), st(mkp), st(mvp), st(cvp),
            st(fks), st(fvs), st(fls), st(sks), st(svs), st(cvs))


_drawn_inputs = setup_inputs


def setup_inputs(seed=0):
    import zlib

    import numpy as np

    out = dict(_drawn_inputs(seed))
    spreads = {}
    factors = {'cache_fox_logf': 2.836, 'swa_sinks': 8.0, 'ln_mem': 3.593, 'b_conv': 3.839}
    for name, (base, spread) in spreads.items():
        noise = np.random.default_rng([zlib.crc32(name.encode()), seed]).standard_normal(out[name].shape)
        drawn = base * np.exp(spread * noise) if base else spread * noise
        out[name] = __import__('jax').numpy.asarray(drawn.astype(out[name].dtype))
    for name, factor in factors.items():
        out[name] = (out[name] * factor).astype(out[name].dtype)
    return out
```

```python
from contextlib import ExitStack, contextmanager

import numpy as np

import concourse.bass as bass
from concourse import mybir

F32 = mybir.dt.float32
F32R = mybir.dt.float32r
ACT = mybir.ActivationFunctionType
ALU = mybir.AluOpType
ds = bass.ds

DEPTH, D, SEQ, DEC, PAST = 2, 1024, 1024, 64, 1024
T = SEQ + DEC
KT = D // 128
FOX_H, HD = 8, 64
SWA_H, SWA_KV = 8, 2
PAIRS = FOX_H // 2
MEM, MEM_H = 256, 4
FF = 2816
FT = FF // 128
NB = SEQ // 128
KEEP = 128
EPS = 1e-6
NEG = -1e30
CH = [(0, 384), (384, 768), (768, T)]
HALF = 512
FOX_SLABS = 10
N_SLABS = 2 + PAIRS * FOX_SLABS + 8 + (4 + PAIRS * 3) + 8 + 16 + MEM_H * 3 + 8 + FT * 6 + 2
assert N_SLABS % 4 == 0
C_MIX, C_MEM, C_TOK, C_FFN = 0, 8, 16, 24
C_CONV = 32
C_BCONV = C_CONV + 3 * FT
C_BF = C_BCONV + FT
C_SINK = C_BF + 1
C_SINK2 = C_SINK + SWA_H
C_STATE = C_SINK2 + PAIRS
N_LC = C_STATE + 2 * FT
N_C8 = SEQ + PAST + DEC


class Place:

    KINDS = ("layer", "slab", "use", "group", "ring", "step", "hi", "self", "store", "norm", "bias", "glu",
             "ntile", "rope", "attn")

    def __init__(self):
        self.n = dict.fromkeys(self.KINDS, 0)
        self.loops = []

    def at(self, kind, more=0, scale=1):
        value = self.n[kind] * scale + more
        for turn, per in self.loops:
            if per[kind]:
                value = turn * (per[kind] * scale) + value
        return value

    def bank_set(self):
        return self.n["use"] % 2

    def set_count(self, more=0):
        value = self.n["use"] // 2 + more
        for turn, per in self.loops:
            if per["use"]:
                value = turn * (per["use"] // 2) + value
        return value

    def uses_of(self, s, more=0):
        value = (self.n["use"] + 1 - s) // 2 + more
        for turn, per in self.loops:
            if per["use"]:
                value = turn * (per["use"] // 2) + value
        return value

    def add(self, kind, k=1):
        self.n[kind] += k


class Silent:

    def __getattr__(self, name):
        return lambda *a, **k: self

    @contextmanager
    def Fori(self, a, b):
        yield 0


def repeat(eng, place, turns, body):
    before = dict(place.n)
    body(Silent(), 0)
    per = {k: place.n[k] - before[k] for k in before}
    assert per["use"] % 2 == 0 and per["group"] % 2 == 0 and per["slab"] % 4 == 0, per
    place.n = dict(before)
    with eng.Fori(0, turns) as turn:
        place.loops.append((turn, per))
        body(eng, turn)
        place.loops.pop()
    place.n = {k: before[k] + turns * per[k] for k in before}


def wait_apart(eng, constant, value, waits):
    held = [(s, v if isinstance(v, int) else eng.to_reg(v)) for s, v in waits]
    eng.wait_ge(constant, value)
    for s, v in held:
        eng.wait_ge(s, v)
    for _, v in held:
        if not isinstance(v, int) and not isinstance(eng, Silent):
            eng.free_register(v)


def encoder_step(nc, xT, memT, slabs, layer_c, final_c, clogf, swa_tail_k, swa_tail_v,
                 o_y, o_fk, o_fv, o_lf, o_sk, o_sv, o_mk, o_mv, o_cv, o_tk, o_tv):
    ctx = ExitStack()
    with ctx:
        def sem(name):
            return ctx.enter_context(nc.semaphore(name))

        at = [(nc.sbuf_base + 31) // 32 * 32]

        def here(name, shape, dt, offset):
            return nc.alloc_sbuf_tensor_at(name, shape, dt, offset=offset)

        def sb(name, shape, dt=F32):
            size = 4 * int(np.prod(shape[1:]))
            offset = at[0]
            at[0] = offset + (size + 31) // 32 * 32
            return here(name, shape, dt, offset)

        XT = sb("XT", [128, KT, T])
        HH0 = at[0]
        HH, HL = (sb(n, [128, KT, T], F32R) for n in ("HH", "HL"))
        RAW = sb("RAW", [128, 4, HALF])
        WH, WL = (sb(n, [128, 4, HALF], F32R) for n in ("WH", "WL"))
        G0H, G0L = (sb(n, [128, 2, T], F32R) for n in ("G0H", "G0L"))
        ident = sb("ident", [128, 128])
        ident_r = sb("ident_r", [128, 128], F32R)
        ones_r = sb("ones_r", [128, 128], F32R)
        causal = sb("causal", [128, 128])
        causal_r = sb("causal_r", [128, 128], F32R)
        tail_mask = sb("tail_mask", [128, DEC])
        tail_mask_r = sb("tail_mask_r", [128, DEC], F32R)
        band = sb("band", [128, 256])
        zero = sb("zero", [128, 256])
        big = sb("big", [128, 1])
        eps = sb("eps", [128, 1])
        one = sb("one", [128, 1])
        LC = sb("LC", [128, N_LC])
        FC = sb("FC", [128, KT])
        NSK = sb("NSK", [128, SWA_H + PAIRS])
        RM = sb("RM", [128, MEM])
        CO = sb("CO", [128, FT * 4])
        NM = sb("NM", [128, 3, 2])
        NM1 = sb("NM1", [128, 1])
        SM = sb("SM", [128, 3, 2])
        ES = sb("ES", [128, 3, 2])
        RC = sb("RC", [128, 3, 2])
        QSH, QSL = (sb(n, [128, 128], F32R) for n in ("QSH", "QSL"))
        U0 = at[0]
        QH, QL = (sb(n, [128, T], F32R) for n in ("QH", "QL"))
        KH0, VH0 = at[0], at[0] + 2 * 4 * T
        KH, KL = (sb(n, [128, T], F32R) for n in ("KH", "KL"))
        VH, VL = (sb(n, [128, 9 * 128], F32R) for n in ("VH", "VL"))
        T32 = sb("T32", [128, T])
        XR0 = at[0]
        XR = sb("XR", [128, 3, T])
        PR0 = at[0]
        PR = sb("PR", [128, 3, T])
        PT0 = at[0]
        PTH, PTL = (sb(n, [128, 3, 512], F32R) for n in ("PTH", "PTL"))
        assert at[0] <= nc.sbuf_top, (at[0], nc.sbuf_top)
        ACC = here("ACC", [128, T], F32, XR0 + 4 * KT * MEM)
        SQ = [here(f"SQ{i}", [128, T], F32, U0 + 4 * T * i) for i in range(2)]
        SH, SL = QH, QL
        assert XR0 + 4 * KT * MEM + 4 * T <= PR0
        FZ = here("FZ", [8, T], F32, KH0)
        FA = here("FA", [8, T], F32, KH0 + 4 * T)
        FL = here("FL", [8, T], F32, VH0)
        CLF = here("CLF", [8, PAST], F32, VH0 + 4 * 1152)
        C8 = here("C8", [8, N_C8], F32, PR0)
        MR = here("MR", [128, KT, MEM], F32, XR0)
        MH = here("MH", [128, KT, MEM], F32R, PR0)
        ML = here("ML", [128, KT, MEM], F32R, PT0)
        MT = here("MT", [128, 2, MEM], F32, U0)
        G1H, G1L = (here(n, [128, 2, T], F32R, U0 + i * 8 * T) for i, n in enumerate(("G1H", "G1L")))
        GP = here("GP", [128, 2, T + 4], F32, U0 + 16 * T)
        YY = here("YY", [128, 2, T + 4], F32, U0 + 16 * T + 8 * (T + 4))
        assert U0 + 16 * T + 16 * (T + 4) <= PR0
        YT = here("YT", [128, KT, T], F32, HH0)
        GH, GL = [G0H, G1H], [G0L, G1L]
        PS = ctx.enter_context(nc.psum_tensor("PS", [128, 8 * 512], F32))
        decays = nc.dram_tensor("decays", [8, N_C8], F32).ap()

        half_hd = HD // 2
        inv = (np.float32(10000.0) ** (-np.arange(half_hd, dtype=np.float32) / np.float32(half_hd))).astype(np.float32)
        angle = (np.arange(T, dtype=np.float32)[:, None] * inv[None, :]).astype(np.float32).T.astype(np.float64)
        cos_t = nc.inline_tensor(np.tile(np.cos(angle), (4, 1)).astype(np.float32), name="cos_t").ap()
        sin_t = nc.inline_tensor(np.concatenate([-np.sin(angle), np.sin(angle)] * 2).astype(np.float32), name="sin_t").ap()
        q, k = np.arange(128)[:, None], np.arange(256)[None, :]
        c_ident = nc.inline_tensor(np.eye(128, dtype=np.float32), name="c_ident").ap()
        c_causal = nc.inline_tensor(np.where(k[:, :128] > q, NEG, 0).astype(np.float32), name="c_causal").ap()
        c_tail = nc.inline_tensor(np.where(k[:, :DEC] > q % DEC, NEG, 0).astype(np.float32), name="c_tail").ap()
        seen = np.where(q < 64, k < 192, k >= 64)
        c_band = nc.inline_tensor(np.where(seen, 0, NEG).astype(np.float32), name="c_band").ap()

        x_in = [sem(f"x_in{i}") for i in range(KT)]
        const_in, mem_in, const_ok, memset_ok = sem("const_in"), sem("mem_in"), sem("const_ok"), sem("memset_ok")
        raw_in = [sem(f"raw_in{i}") for i in range(4)]
        w_hi, w_ready, w_used = sem("w_hi"), sem("w_ready"), sem("w_used")
        full = [sem("full0"), sem("full1")]
        free = [sem("free0"), sem("free1")]
        g_full, g_free = sem("g_full"), sem("g_free")
        hi_done = sem("hi_done")
        act_self, dve_self = sem("act_self"), sem("dve_self")
        e_ready = sem("e_ready")
        p_ready = sem("p_ready")
        p_used = sem("p_used")
        pt_used = sem("pt_used")
        o_full, o_free = sem("o_full"), sem("o_free")
        t32_out = sem("t32_out")
        sq_ready, sq_used = sem("sq_ready"), sem("sq_used")
        stat_ready, attn_ready = sem("stat_ready"), sem("attn_ready")
        ht_ready, h_ready = sem("ht_ready"), sem("h_ready")
        lc_in, ln_done, lf_ready, c_ready, c_stored, lf_out = (sem(n) for n in ("lc_in", "ln_done", "lf_ready", "c_ready", "c_stored", "lf_out"))
        bias_in, trig_in, rope_ready, roped = sem("bias_in"), sem("trig_in"), sem("rope_ready"), sem("roped")
        gate_ready, conv_done, silu_done, glu_ready = sem("gate_ready"), sem("conv_done"), sem("silu_done"), sem("glu_ready")
        co_out = sem("co_out")
        out_done = sem("out_done")
        k32_out = sem("k32_out")
        y_ready = sem("y_ready")

        block = ctx.enter_context(nc.Block())

        def bank(i):
            return PS[:, i * 512:(i + 1) * 512]

        def parts(s):
            b = s * 1536
            two = PS[:, b:b + 1024].rearrange("p (c n) -> p c n", c=2)[:, :, 0:384]
            return [(two, 0, 768), (PS[:, b + 1024:b + 1024 + T - 768], 768, T)]

        def like(ap, a, b):
            return ap[:, a:b].rearrange("p (c n) -> p c n", c=2) if b - a == 768 else ap[:, a:b]

        FOX_SCALE = float(HD) ** -0.5
        MEM_SCALE = float(128) ** -0.5

        def fox_steps():
            steps = []
            for h in range(2):
                for i in range(NB):
                    n = (i + 1) * 128
                    tiles = [(j * 128, 128) for j in range(i + 1)]
                    steps.append(dict(kind="fox", h=h, i=i, width=n, heads=1,
                                      pieces=[("set", 0, 0, n, XR[:, h, 0:n], big, None)],
                                      groups=[tiles[a:a + 4] for a in range(0, i + 1, 4)],
                                      outs=[(64 * h, 64, 0, 64 * h, i * 128, 128)], scale=FOX_SCALE))
            tiles = [(j * 128, 128) for j in range(PAST // 128)]
            steps.append(dict(kind="fox_s", width=PAST + DEC, heads=1,
                              pieces=[("set", 0, 0, PAST, XR[:, 2, 0:PAST], big, None),
                                      ("group", 0, PAST, DEC, XR[:, 2, PAST:T], NM1, None)],
                              groups=[tiles[0:4], tiles[4:8], [(PAST, DEC)]],
                              outs=[(64 * h, 64, 64 * h, 64 * h, SEQ, DEC) for h in range(2)], scale=FOX_SCALE))
            return steps

        def swa_steps(pair):
            steps = []
            kv = 64 * (pair // 2)
            for i in range(NB):
                n = 128 if i == 0 else 256
                steps.append(dict(kind="swa", i=i, pair=pair, width=512, heads=2,
                                  pieces=[("set", 512 * h, 256 * h, n, band[:, 256 - n:256],
                                           NSK[:, 2 * pair + h:2 * pair + h + 1], 2 * pair + h) for h in range(2)],
                                  groups=[[(256 * h + 128 * j, 128) for h in range(2) for j in range(n // 128)]],
                                  outs=[(kv, 64, 128 * h, 64 * h, i * 128, 128) for h in range(2)], scale=FOX_SCALE))
            steps.append(dict(kind="swa_s", pair=pair, width=KEEP + DEC, heads=1,
                              pieces=[("set", 0, 0, KEEP + DEC, zero[:, 0:KEEP + DEC],
                                       NSK[:, SWA_H + pair:SWA_H + pair + 1], SWA_H + pair)],
                              groups=[[(0, 128), (128, DEC)]],
                              outs=[(kv, 64, 64 * h, 64 * h, SEQ, DEC) for h in range(2)], scale=FOX_SCALE))
            return steps

        def mem_steps(head):
            steps = [dict(kind="mem", i=i, head=head, width=MEM, heads=1,
                          pieces=[("set", 0, 0, MEM, zero[:, 0:MEM], big, None)],
                          groups=[[(0, 128), (128, 128)]],
                          outs=[(0, 128, 0, 0, i * 128, 128)], scale=MEM_SCALE) for i in range(NB)]
            steps.append(dict(kind="mem_s", head=head, width=MEM, heads=1,
                              pieces=[("set", 0, 0, MEM, zero[:, 0:MEM], big, None)],
                              groups=[[(0, 128), (128, 128)]],
                              outs=[(0, 128, 0, 0, SEQ, DEC)], scale=MEM_SCALE))
            return steps

        V_GROUPS = [[0, 1, 2], [3, 4], [5, 6], [7, 8]]

        def group_areas(tiles):
            whole = [j for j, (_, rows) in enumerate(tiles) if rows == 128]
            areas = [(128, 0, 128 * len(whole))] if whole else []
            return areas + [(rows, 128 * j, 128) for j, (_, rows) in enumerate(tiles) if rows < 128]

        @block.sync
        def _(sp):
            sp.dma_start(MR[:, :, :], memT).then_inc(mem_in, 16)
            for kt in range(KT):
                sp.dma_start(XT[:, kt, :], xT[:, kt, :]).then_inc(x_in[kt], 16)
            for a, b in ((ident, c_ident), (causal, c_causal), (tail_mask, c_tail), (band, c_band), (FC, final_c)):
                sp.dma_start(a[:], b).then_inc(const_in, 16)
            for s in range(4):
                sp.dma_start(RAW[:, s, :], slabs[s]).then_inc(raw_in[s], 16)
            with sp.Fori(1, DEPTH * N_SLABS // 4) as turn:
                for s in range(4):
                    sp.wait_ge(w_ready, turn * 4 + (s - 3))
                    sp.dma_start(RAW[:, s, :], slabs[ds(turn * 4 + s, 1)].rearrange("o p n -> p (o n)")).then_inc(raw_in[s], 16)
            for l in range(DEPTH):
                sp.dma_start(o_tk[l], swa_tail_k[l]).then_inc(out_done, 16)
                sp.dma_start(o_tv[l], swa_tail_v[l]).then_inc(out_done, 16)
            sp.wait_ge(out_done, 16 * (2 * DEPTH + KT))
            sp.wait_ge(lf_out, 16 * DEPTH)
            sp.wait_ge(k32_out, 16 * DEPTH)
            sp.wait_ge(t32_out, 16 + 16 * DEPTH * (2 * PAIRS + 1 + 2 * MEM_H))
            sp.wait_ge(co_out, 16 + 16 * DEPTH)

        @block.gpsimd
        def _(pool):
            pool.memset(zero[:], 0.0).then_inc(memset_ok, 1)
            pool.memset(big[:], 3.0e38).then_inc(memset_ok, 1)
            pool.memset(eps[:], EPS).then_inc(memset_ok, 1)
            pool.memset(one[:], 1.0).then_inc(memset_ok, 1)

            def split(turn, s):
                pool.wait_ge(raw_in[s], turn * 16 + 16)
                if not isinstance(turn, int):
                    pool.wait_ge(w_used, turn * 4 + (s - 3))
                pool.tensor_tensor(WH[:, s, :], RAW[:, s, :], zero[:, 0:1].to_broadcast([128, HALF]), ALU.add).then_inc(w_hi, 1)
                pool.wait_ge(w_hi, turn * 4 + (s + 1))
                pool.tensor_tensor(WL[:, s, :], RAW[:, s, :], WH[:, s, :].bitcast(F32), ALU.subtract).then_inc(w_ready, 1)

            pool.wait_ge(memset_ok, 4)
            for s in range(4):
                split(0, s)
            with pool.Fori(1, DEPTH * N_SLABS // 4) as turn:
                for s in range(4):
                    split(turn, s)

        @block.tensor
        def _(pe0):
            place = Place()
            pe0.wait_ge(const_ok, 5)
            pe0.wait_ge(const_in, 80)
            pe0.sem_inc(p_used, 3)
            pe0.sem_inc(pt_used, 3)
            held_groups = []
            owed = []
            state = {"last": None, "bare": False}

            def mm(pe, *a, transpose=False, **k):
                ins = pe.transpose(*a) if transpose else pe.matmul(*a, **k)
                state["last"], state["bare"] = ins, not owed
                if owed:
                    ins.then_inc(owed.pop(0), 1)

            def signal(s, now=False):
                if state["bare"]:
                    state["last"].then_inc(s, 1)
                    state["bare"] = False
                else:
                    assert not now
                    owed.append(s)

            def claim(pe, banks):
                s = place.bank_set()
                pe.wait_ge(free[s], place.set_count(1))
                if banks == 3:
                    pe.wait_ge(o_free, place.at("step", 2))
                return s

            def done(s):
                signal(full[s], now=True)
                place.add("use")

            def slab(pe):
                slot = place.n["slab"] % 4
                pe.wait_ge(w_ready, place.at("slab", 1))
                place.add("slab")
                return slot

            def project(pe, xh, xl, chunks, fresh=None):
                s = claim(pe, 3)
                for half in range(2):
                    slot = slab(pe)
                    for k in range(4):
                        kt = half * 4 + k
                        if fresh is not None:
                            pe.wait_ge(h_ready, place.at("ntile", fresh + kt + 1))
                        for w, x in ((WH, xh), (WH, xl), (WL, xh)):
                            for c, (a, b) in enumerate(chunks):
                                o = s * 1536 + c * 512
                                mm(pe, PS[:, o:o + b - a], w[:, slot, k * 128:(k + 1) * 128], x[:, kt, a:b],
                                   start=(kt == 0 and w is WH and x is xh), stop=(kt == KT - 1 and w is WL))
                    if half == 0:
                        signal(w_used, now=True)
                done(s)
                signal(w_used)

            def down(pe, b):
                slots = None
                for m in range(KT):
                    s = claim(pe, 3)
                    if m % 4 == 0:
                        slots = [slab(pe), slab(pe)]
                    for r in range(2):
                        for w, x in ((WH, GH[b]), (WH, GL[b]), (WL, GH[b])):
                            for c, (a0, b0) in enumerate(CH):
                                o = s * 1536 + c * 512
                                mm(pe, PS[:, o:o + b0 - a0], w[:, slots[r], (m % 4) * 128:(m % 4 + 1) * 128],
                                   x[:, r, a0:b0], start=(r == 0 and w is WH and x is GH[b]), stop=(r == 1 and w is WL))
                        if m % 4 == 3 and r == 0:
                            signal(w_used, now=True)
                    done(s)
                    if m % 4 == 3:
                        signal(w_used)

            def stat(pe, width):
                s = claim(pe, 3)
                pe.wait_ge(stat_ready, place.at("norm", 1))
                for x in (SH, SL):
                    for c, (a, b) in enumerate(CH if width == T else [(0, width)]):
                        o = s * 1536 + c * 512
                        mm(pe, PS[:, o:o + b - a], ones_r[:], x[:, a:b], start=(x is SH), stop=(x is SL))
                done(s)
                place.add("norm")

            def value_tiles(pe, tiles_of, rows_of):
                place.add("use", -1)
                pe.wait_ge(free[place.bank_set()], place.set_count(2))
                place.add("use", 1)
                for tiles in tiles_of:
                    wait_apart(pe, const_in, 80, [(g_free, place.at("group", 1))])
                    b = 6 + place.n["group"] % 2
                    for j, tile in enumerate(tiles):
                        rows = rows_of(tile)
                        mm(pe, PS[0:rows, b * 512 + j * 128:b * 512 + (j + 1) * 128],
                           T32[:, tile * 128:tile * 128 + rows], ident[:], transpose=True)
                    signal(g_full, now=True)
                    place.add("group")

            def scores(pe, st, held):
                s = claim(pe, 2)
                o = s * 1536

                def product(out, width, lh, ll, rh, rl, mask=None):
                    for a, b, last in ((lh, rh, False), (lh, rl, False), (ll, rh, True)):
                        for c in range(0, width, 512):
                            e = min(width, c + 512)
                            mm(pe, PS[:, out + c:out + e], a, b[:, c:e], start=(a is lh and b is rh),
                               stop=last and not (mask is not None and e == width))
                    if mask is not None:
                        n = mask.shape[1]
                        mm(pe, PS[:, out + width - n:out + width], ident_r[:], mask[:], start=False, stop=True)

                if st["kind"] == "fox":
                    r, i, n = slice(64 * st["h"], 64 * st["h"] + 64), st["i"], st["width"]
                    product(o, n, QH[r, i * 128:(i + 1) * 128], QL[r, i * 128:(i + 1) * 128], KH[r, 0:n], KL[r, 0:n], causal_r)
                elif st["kind"] == "fox_s":
                    slots = [slab(pe), slab(pe)]
                    for j in range(2):
                        product(o + 512 * j, 512, QSH[:], QSL[:], WH[:, slots[j], :], WL[:, slots[j], :])
                elif st["kind"] == "swa":
                    i = st["i"]
                    a = max(0, i - 1) * 128
                    for h in range(2):
                        r = slice(64 * h, 64 * h + 64)
                        product(o + 512 * h, (i + 1) * 128 - a, QH[r, i * 128:(i + 1) * 128], QL[r, i * 128:(i + 1) * 128],
                                KH[r, a:(i + 1) * 128], KL[r, a:(i + 1) * 128])
                elif st["kind"] == "swa_s":
                    slot = slab(pe)
                    held["v"] = slot
                    product(o, KEEP, QSH[:], QSL[:], WH[:, slot, 0:KEEP], WL[:, slot, 0:KEEP])
                    product(o + KEEP, DEC, QSH[:], QSL[:], KH[:, SEQ:T], KL[:, SEQ:T])
                elif st["kind"] == "mem":
                    i, h = st["i"], st["head"]
                    product(o, MEM, QH[:, i * 128:(i + 1) * 128], QL[:, i * 128:(i + 1) * 128],
                            KH[:, h * MEM:(h + 1) * MEM], KL[:, h * MEM:(h + 1) * MEM])
                else:
                    slot = slab(pe)
                    held["v"] = slot
                    product(o, MEM, QH[:, T - 128:T], QL[:, T - 128:T], WH[:, slot, 0:MEM], WL[:, slot, 0:MEM])
                done(s)
                if st["kind"] == "fox_s":
                    signal(w_used)
                    signal(w_used)
                    pe.wait_ge(g_free, place.at("group", 1))
                    b = (6 + place.n["group"] % 2) * 512
                    product(b, DEC, QSH[:], QSL[:], KH[:, SEQ:T], KL[:, SEQ:T], tail_mask_r)
                    signal(g_full, now=True)
                    place.add("group")

            def transposes(pe, st, s, first):
                pe.wait_ge(p_ready, place.at("step", s + 1))
                for tiles in st["groups"]:
                    wait_apart(pe, const_in, 80, [(g_free, place.at("group", 1))])
                    b = 6 + place.n["group"] % 2
                    for j, (col, rows) in enumerate(tiles):
                        mm(pe, PS[0:rows, b * 512 + j * 128:b * 512 + (j + 1) * 128],
                           PR[:, s % 3, col:col + rows], ident[:], transpose=True)
                    signal(g_full, now=True)
                    held_groups.append(place.at("group", 3))
                    place.add("group")
                signal(p_used)

            def values(pe, st, s, ring, held):
                o = (2 + 3 * (s % 2)) * 512
                pe.wait_ge(o_free, place.at("step", s + 1))
                tile = 0
                n_tiles = sum(len(g) for g in st["groups"])
                for gi, tiles in enumerate(st["groups"]):
                    pe.wait_ge(g_free, held_groups[ring + gi])
                    slot = (ring + gi) % 3
                    held_slot = None
                    if st["kind"] == "fox_s" and gi < 2:
                        held_slot = slab(pe)
                    for j, (col, rows) in enumerate(tiles):
                        out, n, q0, first, last = o, 128, 0, tile == 0, tile == n_tiles - 1
                        if st["kind"] == "fox" or (st["kind"] == "fox_s" and rows < 128):
                            v = [x[0:rows, tile * 128:(tile + 1) * 128] for x in (VH, VL)]
                        elif st["kind"] == "fox_s":
                            v = [x[:, held_slot, j * 128:(j + 1) * 128] for x in (WH, WL)]
                        elif st["kind"] == "swa":
                            per = n_tiles // 2
                            h, kt = tile // per, max(0, st["i"] - 1) + tile % per
                            v = [x[:, kt * 128:(kt + 1) * 128] for x in (VH, VL)]
                            out, first, last = o + 128 * h, tile % per == 0, tile % per == per - 1
                        elif st["kind"] == "swa_s":
                            if tile == 0:
                                v = [x[:, held["v"], KEEP:2 * KEEP] for x in (WH, WL)]
                            else:
                                v = [x[0:rows, 8 * 128:9 * 128] for x in (VH, VL)]
                        elif st["kind"] == "mem":
                            c = (st["head"] * 2 + tile) * 128
                            v = [x[:, c:c + 128] for x in (VH, VL)]
                        else:
                            c = MEM + tile * 128
                            v = [x[:, held["v"], c:c + 128] for x in (WH, WL)]
                            n, q0 = DEC, 64
                        p = [x[0:rows, slot, j * 128 + q0:j * 128 + q0 + n] for x in (PTH, PTL)]
                        for a, b, k in ((0, 0, 0), (0, 1, 1), (1, 0, 2)):
                            mm(pe, PS[:, out:out + n], v[a], p[b], start=(first and k == 0), stop=(last and k == 2))
                        tile += 1
                    if gi == len(st["groups"]) - 1:
                        signal(o_full, now=True)
                    signal(pt_used)
                    if held_slot is not None:
                        signal(w_used)
                if st["kind"] in ("swa_s", "mem_s"):
                    signal(w_used)

            def attention(pe, steps):
                pe.wait_ge(attn_ready, place.at("attn", 1))
                place.add("attn")
                held_groups.clear()
                rings = [0]
                for st in steps:
                    rings.append(rings[-1] + len(st["groups"]))
                held = {}
                for s in range(len(steps) + 3):
                    if s < len(steps):
                        scores(pe, steps[s], held)
                    if 2 <= s < len(steps) + 2:
                        transposes(pe, steps[s - 2], s - 2, None)
                    if s >= 3:
                        values(pe, steps[s - 3], s - 3, rings[s - 3], held)
                place.add("step", len(steps))
                place.add("ring", rings[-1])

            def own_values(tile):
                return 128 if tile < NB else DEC

            pe0.wait_ge(memset_ok, 4)
            stat(pe0, MEM)

            def layer(pe, l):
                stat(pe, T)
                project(pe, HH, HL, CH, fresh=0)
                place.add("ntile", KT)

                def fox(pe, turn):
                    for _ in range(2):
                        for _ in range(3):
                            project(pe, HH, HL, CH)
                        value_tiles(pe, V_GROUPS, own_values)
                        attention(pe, fox_steps())
                    pe.wait_ge(o_free, place.at("step", 2))
                    down(pe, 0)

                repeat(pe, place, 2, fox)
                project(pe, HH, HL, CH)
                project(pe, HH, HL, CH)
                value_tiles(pe, V_GROUPS, own_values)
                for pair in range(PAIRS):
                    project(pe, HH, HL, CH)
                    attention(pe, swa_steps(pair))
                    if pair % 2:
                        pe.wait_ge(o_free, place.at("step", 2))
                        down(pe, 0)
                for m in range(2 * MEM_H):
                    project(pe, MH, ML, [(0, MEM)], fresh=0)
                    if m >= MEM_H:
                        value_tiles(pe, [[0, 1]], lambda tile: 128)
                place.add("ntile", KT)
                stat(pe, T)
                for head in range(MEM_H):
                    project(pe, HH, HL, CH, fresh=0)
                    attention(pe, mem_steps(head))
                    if head % 2:
                        pe.wait_ge(o_free, place.at("step", 2))
                        down(pe, 0)
                place.add("ntile", KT)
                stat(pe, T)

                def up(pe):
                    for _ in range(4):
                        project(pe, HH, HL, CH, fresh=0)

                def mix_down(pe, b):
                    pe.wait_ge(glu_ready, place.at("glu", 2))
                    down(pe, b)
                    place.add("glu", 2)

                up(pe)

                def mixer(pe, turn):
                    for b in range(2):
                        up(pe)
                        mix_down(pe, b)

                repeat(pe, place, (FT // 2 - 1) // 2, mixer)
                mix_down(pe, 0)
                place.add("ntile", KT)
                place.add("slab", 2)
                assert owed == [w_used]
                owed.clear()
                pe.drain().then_inc(w_used, 3)
                place.add("layer")

            repeat(pe0, place, DEPTH, layer)
            stat(pe0, T)

        def wait_all_read(eng, place):
            eng.wait_ge(free[0], place.uses_of(0, 1))
            eng.wait_ge(free[1], place.uses_of(1, 1))

        def wait_read(eng, place):
            eng.wait_ge(free[place.bank_set()], place.set_count(2))

        def wait_full(eng, place):
            eng.wait_ge(full[place.bank_set()], place.set_count(1))

        def step_areas(st):
            if st["heads"] == 1:
                return [(0, st["width"])]
            return [(p, p + n) for _, _, p, n, _, _, _ in st["pieces"]]

        @block.scalar
        def _(act0):
            place = Place()
            act0.sem_inc(t32_out, 16)
            act0.sem_inc(co_out, 16)

            def copy(act, out, in_):
                return act.activation(out, in_, ACT.Copy)

            def wait_own(act, ins):
                ins.then_inc(act_self, 1)
                place.add("self")
                act.wait_ge(act_self, place.at("self"))

            def hi(act, pieces):
                for out, in_ in pieces:
                    ins = copy(act, out, in_)
                ins.then_inc(hi_done, 1)

            def hi_tile(act, out):
                hi(act, [(like(out, a, b), src) for src, a, b in parts(place.bank_set())])

            def fill_t32(act, width=T):
                act.wait_ge(t32_out, place.at("store", 16, 16))
                if width == T:
                    for src, a, b in parts(place.bank_set()):
                        ins = copy(act, like(T32, a, b), src)
                else:
                    o = place.bank_set() * 1536
                    ins = copy(act, T32[:, 0:width], PS[:, o:o + width])
                return ins

            def store_t32(act, out, a, b):
                act.dma_start(out, T32[:, a:b]).then_inc(t32_out, 16)
                place.add("store")

            def group_hi(act, tiles_areas, out):
                act.wait_ge(g_full, place.at("group", 1))
                b = (6 + place.n["group"] % 2) * 512
                hi(act, [(out[0:rows, c:c + n], PS[0:rows, b + c:b + c + n]) for rows, c, n in tiles_areas])
                place.add("group")

            def value_groups(act, groups, rows_of, first=0):
                for tiles in groups:
                    areas = group_areas([(0, rows_of(t)) for t in tiles])
                    group_hi(act, areas, VH[:, (first + tiles[0]) * 128:])

            def squares(act, m, ready):
                ready()
                if m >= 3:
                    act.wait_ge(sq_used, place.at("norm", m - 2, 7))
                return ACC if m == 0 else SQ[m % 2]

            def split_sums(act, width):
                act.wait_ge(sq_used, place.at("norm", 7, 7))
                hi(act, [(SH[:, 0:width], ACC[:, 0:width])])

            def deviations(act, out, width):
                wait_full(act, place)
                if width == T:
                    for src, a, b in parts(place.bank_set()):
                        ins = act.activation(like(out, a, b), src, ACT.Sqrt, bias=eps[:], scale=1.0 / D)
                else:
                    o = place.bank_set() * 1536
                    ins = act.activation(out[:, 0:width], PS[:, o:o + width], ACT.Sqrt, bias=eps[:], scale=1.0 / D)
                ins.then_inc(free[place.bank_set()], 1)
                place.add("use")
                place.add("norm")

            def normalised_hi(act, dst, tmp):
                for kt in range(KT):
                    act.wait_ge(ht_ready, place.at("ntile", kt + 1))
                    hi(act, [(dst[:, kt, :], tmp(kt))])
                place.add("ntile", KT)

            def attention(act, steps, r):
                n = len(steps)
                for s in range(n + 3):
                    if s < n:
                        st = steps[s]
                        wait_read(act, place)
                        place.add("use")
                        if st["kind"] == "fox_s":
                            act.wait_ge(g_free, place.at("group", 3))
                            place.add("group")
                        for h, (a, b) in enumerate(step_areas(st)):
                            sink = st["pieces"][h][6]
                            if sink is not None:
                                act.activation(ES[:, s % 3, h:h + 1], NSK[:, sink:sink + 1], ACT.Exp,
                                               bias=NM[:, s % 3, h:h + 1], scale=-1.0)
                            ins = act.activation(PR[:, s % 3, a:b], PR[:, s % 3, a:b], ACT.Exp,
                                                 bias=NM[:, s % 3, h:h + 1], scale=-1.0, accum_out=SM[:, s % 3, h:h + 1])
                        ins.then_inc(e_ready, 1)
                    if 2 <= s < n + 2:
                        for tiles in steps[s - 2]["groups"]:
                            act.wait_ge(pt_used, place.at("ring", 1))
                            slot = ring[0] % 3
                            group_hi(act, group_areas(tiles), PTH[:, slot, :])
                            ring[0] += 1
                            place.add("ring")
                    if s >= 3:
                        act.wait_ge(o_full, place.at("step", s - 2))
                        o = (2 + 3 * ((s - 3) % 2)) * 512
                        hi(act, [(G0H[g:g + rows, r, t:t + m], PS[p:p + rows, o + c:o + c + m])
                                 for p, rows, c, g, t, m in steps[s - 3]["outs"]])
                place.add("step", n)
                ring[0] = 0

            ring = [0]

            def down(act, with_squares):
                for m in range(KT):
                    if with_squares:
                        dst = squares(act, m, lambda: wait_read(act, place))
                        act.activation(dst[:], XT[:, m, :], ACT.Square).then_inc(sq_ready, 1)
                    place.add("use")
                if with_squares:
                    split_sums(act, T)

            def rope_swap(act):
                wait_full(act, place)
                for src, a, b in parts(place.bank_set()):
                    for g in range(4):
                        p, w = 32 * g, 32 * (g ^ 1)
                        ins = copy(act, like(PR[p:p + 32, 0, :], a, b), src[w:w + 32])
                ins.then_inc(rope_ready, 1)
                place.add("use")
                place.add("rope")

            act0.wait_ge(memset_ok, 4)
            act0.wait_ge(mem_in, 16)
            for m in range(KT):
                dst = squares(act0, m, lambda: None)
                act0.activation(dst[:, 0:MEM], MR[:, m, :], ACT.Square).then_inc(sq_ready, 1)
            split_sums(act0, MEM)
            deviations(act0, RM, MEM)
            for m in range(KT):
                dst = squares(act0, m, lambda: act0.wait_ge(x_in[m], 16))
                act0.activation(dst[:], XT[:, m, :], ACT.Square).then_inc(sq_ready, 1)
            split_sums(act0, T)

            def layer(act, l):
                wait_all_read(act, place)
                act.dma_start(LC[:], layer_c[ds(l, 1)].rearrange("o p n -> p (o n)")).then_inc(lc_in, 16)
                act.dma_start(CLF[:], clogf[ds(l, 1)].rearrange("o p n -> p (o n)")).then_inc(lc_in, 16)
                deviations(act, PR[:, 0, :], T)
                normalised_hi(act, HH, lambda kt: PR[:, 1 + kt % 2, :])

                act.wait_ge(lc_in, place.at("layer", 32, 32))
                wait_full(act, place)
                for src, a, b in parts(place.bank_set()):
                    ins = act.activation(like(FZ, a, b), src[0:8], ACT.Identity, bias=LC[0:8, C_BF:C_BF + 1])
                ins.then_inc(free[place.bank_set()], 1)
                wait_read(act, place)
                place.add("use")
                wait_own(act, act.activation(FA[:], FZ[:], ACT.Abs))
                wait_own(act, act.activation(FA[:], FA[:], ACT.Exp, scale=-1.0))
                act.activation(FA[:], FA[:], ACT.Ln, bias=one[0:8, :]).then_inc(ln_done, 1)
                act.wait_ge(lf_ready, place.at("layer", 1))
                act.dma_start(o_lf[ds(l, 1)].rearrange("o p n -> p (o n)"), FL[:]).then_inc(lf_out, 16)
                act.wait_ge(c_ready, place.at("layer", 1))
                act.dma_start(decays, C8[:]).then_inc(c_stored, 16)

                def fox(act, turn):
                    for half in range(2):
                        pair = turn * 2 + half
                        wait_all_read(act, place)
                        act.wait_ge(c_stored, place.at("layer", 16, 16))
                        act.wait_ge(lf_out, place.at("layer", 16, 16))
                        for h in range(2):
                            row = decays[ds(pair * 2 + h, 1), :]
                            act.dma_start(XR[:, h, 0:SEQ], row[:, 0:SEQ].to_broadcast([128, SEQ])).then_inc(bias_in, 16)
                            act.dma_start(XR[64 * h:64 * h + 64, 2, :], row[:, SEQ:N_C8].to_broadcast([64, T])).then_inc(bias_in, 16)
                        wait_full(act, place)
                        hi_tile(act, QH)
                        place.add("use")
                        wait_full(act, place)
                        ins = fill_t32(act)
                        ins.then_inc(act_self, 1)
                        place.add("self")
                        hi_tile(act, KH)
                        act.wait_ge(act_self, place.at("self"))
                        store_t32(act, o_fk[ds(l * PAIRS + pair, 1)].rearrange("o p n -> p (o n)"), 0, T)
                        place.add("use")
                        wait_full(act, place)
                        fill_t32(act).then_inc(free[place.bank_set()], 1)
                        wait_read(act, place)
                        place.add("use")
                        store_t32(act, o_fv[ds(l * PAIRS + pair, 1)].rearrange("o p n -> p (o n)"), 0, T)
                        value_groups(act, V_GROUPS, lambda t: 128 if t < NB else DEC)
                        attention(act, fox_steps(), half)
                    down(act, False)

                repeat(act, place, 2, fox)

                wait_all_read(act, place)
                act.dma_start(XR[:, 0, :], cos_t).then_inc(trig_in, 16)
                act.dma_start(XR[:, 1, :], sin_t).then_inc(trig_in, 16)
                rope_swap(act)
                act.wait_ge(roped, place.at("rope"))
                act.dma_start(o_sk[ds(l, 1)].rearrange("o p n -> p (o n)"), XR[:, 2, SEQ - KEEP:T]).then_inc(k32_out, 16)
                wait_full(act, place)
                fill_t32(act).then_inc(free[place.bank_set()], 1)
                wait_read(act, place)
                place.add("use")
                store_t32(act, o_sv[ds(l, 1)].rearrange("o p n -> p (o n)"), SEQ - KEEP, T)
                value_groups(act, V_GROUPS, lambda t: 128 if t < NB else DEC)
                for pair in range(PAIRS):
                    rope_swap(act)
                    if pair % 2 == 0:
                        act.wait_ge(t32_out, place.at("store", 16, 16))
                        g = 64 * (pair // 2)
                        copy(act, T32[0:64, :], XR[g:g + 64, 2, :])
                        wait_own(act, copy(act, T32[64:128, :], XR[g:g + 64, 2, :]))
                        hi(act, [(KH[:], T32[:])])
                    act.wait_ge(roped, place.at("rope"))
                    hi(act, [(QH[:], PR[:, 2, :])])
                    if pair == PAIRS - 1:
                        act.wait_ge(k32_out, place.at("layer", 16, 16))
                        act.dma_start(MR[:, :, :], memT).then_inc(mem_in, 16)
                    attention(act, swa_steps(pair), pair % 2)
                    if pair == PAIRS - 1:
                        normalised_hi(act, MH, lambda kt: MT[:, kt % 2, :])
                    if pair % 2:
                        down(act, pair == PAIRS - 1)

                for m in range(2 * MEM_H):
                    wait_full(act, place)
                    ins = fill_t32(act, MEM)
                    o = place.bank_set() * 1536
                    h = m % MEM_H
                    out = (o_mk if m < MEM_H else o_mv)[ds(l * MEM_H + h, 1)].rearrange("o p n -> p (o n)")
                    if m < MEM_H:
                        ins.then_inc(act_self, 1)
                        place.add("self")
                        hi(act, [(KH[:, h * MEM:(h + 1) * MEM], PS[:, o:o + MEM])])
                        act.wait_ge(act_self, place.at("self"))
                    else:
                        ins.then_inc(free[place.bank_set()], 1)
                        wait_read(act, place)
                    place.add("use")
                    store_t32(act, out, 0, MEM)
                    if m >= MEM_H:
                        value_groups(act, [[0, 1]], lambda t: 128, first=2 * h)
                deviations(act, PR[:, 0, :], T)
                normalised_hi(act, HH, lambda kt: PR[:, 1 + kt % 2, :])
                for head in range(MEM_H):
                    wait_full(act, place)
                    hi_tile(act, QH)
                    place.add("use")
                    attention(act, mem_steps(head), head % 2)
                    if head % 2:
                        down(act, head == MEM_H - 1)
                deviations(act, PR[:, 0, :], T)
                normalised_hi(act, HH, lambda kt: PR[:, 1 + kt % 2, :])

                act.wait_ge(co_out, place.at("layer", 16, 16))
                act.wait_ge(t32_out, place.at("store", 16, 16))

                def gates(act, f, g):
                    for r in range(2):
                        s = place.bank_set()
                        b = s * 1536
                        act.wait_ge(conv_done, place.at("glu", r + 1))
                        wait_full(act, place)
                        two, _, _ = parts(s)[0]
                        copy(act, GP[:, r, 2:770].rearrange("p (c n) -> p c n", c=2), two)
                        copy(act, GP[:, r, 770:2 + SEQ], PS[:, b + 1024:b + 1024 + SEQ - 768])
                        copy(act, GP[:, r, SEQ + 4:T + 4], PS[:, b + 1024 + SEQ - 768:b + 1024 + T - 768])
                        copy(act, CO[:, ds((f + r) * 4, 2)], PS[:, b + 1024 + SEQ - 770:b + 1024 + SEQ - 768])
                        copy(act, CO[:, ds((f + r) * 4 + 2, 2)], PS[:, b + 1024 + T - 770:b + 1024 + T - 768])\
                            .then_inc(free[s], 1)
                        copy(act, GP[:, r, SEQ + 2:SEQ + 4], LC[:, ds((f + r) * 2 + C_STATE, 2)]).then_inc(gate_ready, 1)
                        place.add("use")
                        act.wait_ge(conv_done, place.at("glu", r + 3))
                        act.activation(YY[:, r, 0:T + 2], YY[:, r, 0:T + 2], ACT.Silu).then_inc(silu_done, 1)
                        wait_read(act, place)
                        place.add("use")
                        hi(act, [(GH[g][:, r, 0:SEQ], YY[:, r, 0:SEQ]), (GH[g][:, r, SEQ:T], YY[:, r, SEQ + 2:T + 2])])
                    place.add("glu", 2)

                gates(act, 0, 0)

                def mixer(act, turn):
                    for b in range(2):
                        gates(act, turn * 4 + 2 * (b + 1), 1 - b)
                        down(act, False)

                repeat(act, place, (FT // 2 - 1) // 2, mixer)
                act.dma_start(o_cv[ds(l, 1)].rearrange("o p n -> p (o n)"), CO[:]).then_inc(co_out, 16)
                down(act, True)
                place.add("layer")

            repeat(act0, place, DEPTH, layer)
            deviations(act0, PR[:, 0, :], T)
            for kt in range(KT):
                act0.wait_ge(y_ready, kt + 1)
                act0.dma_start(o_y[:, kt, :], YT[:, kt, :]).then_inc(out_done, 16)

        @block.vector
        def _(dve0):
            place = Place()
            dve0.sem_inc(free[0], 1)
            dve0.sem_inc(free[1], 1)
            dve0.sem_inc(g_free, 2)
            dve0.sem_inc(o_free, 2)
            dve0.sem_inc(conv_done, 2)
            dve0.wait_ge(const_in, 80)
            dve0.tensor_copy(ident_r[:], ident[:]).then_inc(const_ok, 1)
            dve0.tensor_copy(causal_r[:], causal[:]).then_inc(const_ok, 1)
            dve0.tensor_copy(tail_mask_r[:], tail_mask[:]).then_inc(const_ok, 1)
            dve0.tensor_scalar(ones_r[:], ident[:], 0.0, 1.0, ALU.mult, ALU.add).then_inc(const_ok, 1)
            dve0.memset(QSH[:].bitcast(F32), 0.0).then_inc(dve_self, 1)
            dve0.memset(QSL[:].bitcast(F32), 0.0).then_inc(const_ok, 1)
            dve0.wait_ge(memset_ok, 4)
            place.add("self")

            def wait_own(dve, ins):
                ins.then_inc(dve_self, 1)
                place.add("self")
                dve.wait_ge(dve_self, place.at("self"))

            def lo(dve, pieces):
                dve.wait_ge(hi_done, place.at("hi", 1))
                place.add("hi")
                for out, in_, high in pieces:
                    ins = dve.tensor_tensor(out, in_, high.bitcast(F32), ALU.subtract)
                return ins

            def lo_tile(dve, low, high):
                lo(dve, [(like(low, a, b), src, like(high, a, b)) for src, a, b in parts(place.bank_set())])\
                    .then_inc(free[place.bank_set()], 1)
                place.add("use")

            def group_lo(dve, areas, low, high):
                b = (6 + place.n["group"] % 2) * 512
                lo(dve, [(low[0:rows, c:c + n], PS[0:rows, b + c:b + c + n], high[0:rows, c:c + n]) for rows, c, n in areas])\
                    .then_inc(g_free, 1)
                place.add("group")

            def value_groups(dve, groups, rows_of, first=0):
                for tiles in groups:
                    areas = group_areas([(0, rows_of(t)) for t in tiles])
                    c = (first + tiles[0]) * 128
                    group_lo(dve, areas, VL[:, c:], VH[:, c:])

            def sample_queries(dve):
                wait_all_read(dve, place)
                for out, src in ((QSH, QH), (QSL, QL)):
                    for h in range(2):
                        r = slice(64 * h, 64 * h + 64)
                        ins = dve.tensor_copy(out[r, r], src[r, SEQ:T].bitcast(F32))
                ins.then_inc(attn_ready, 1)
                place.add("attn")

            def add_square(dve, m, width=T):
                dve.wait_ge(sq_ready, place.at("norm", m + 1, 8))
                if m > 1:
                    dve.wait_ge(sq_used, place.at("norm", m - 1, 7))
                dve.tensor_tensor(ACC[:, 0:width], ACC[:, 0:width], SQ[m % 2][:, 0:width], ALU.add).then_inc(sq_used, 1)

            def split_sums(dve, width):
                lo(dve, [(SL[:, 0:width], ACC[:, 0:width], SH[:, 0:width])]).then_inc(stat_ready, 1)

            def inverse(dve, out, width):
                wait_read(dve, place)
                place.add("use")
                place.add("norm")
                wait_own(dve, dve.reciprocal(out[:, 0:width], out[:, 0:width]))

            def normalised(dve, src, gains, scale, tmp, high, low):
                for kt in range(KT + 1):
                    if kt < KT:
                        if kt >= 2:
                            dve.wait_ge(h_ready, place.at("ntile", kt - 1))
                        dve.scalar_tensor_tensor(tmp(kt), src(kt), gains[:, kt:kt + 1], scale, ALU.mult, ALU.mult)\
                            .then_inc(ht_ready, 1)
                    if kt >= 1:
                        j = kt - 1
                        lo(dve, [(low[:, j, :], tmp(j), high[:, j, :])]).then_inc(h_ready, 1)
                place.add("ntile", KT)

            def attention(dve, steps, r):
                n = len(steps)
                for s in range(n + 3):
                    if s < n:
                        st = steps[s]
                        o = place.bank_set() * 1536
                        waits = [(full[place.bank_set()], place.set_count(1))]
                        if s == 0 and st["kind"] == "fox":
                            place.add("bias")
                            waits.append((bias_in, place.at("bias", 0, 64)))
                        if s >= 3:
                            waits.append((p_used, place.at("step", s + 1)))
                        wait_apart(dve, memset_ok, 4, waits)
                        heads = 0
                        for j, (where, c, p, m, bias, start, _) in enumerate(st["pieces"]):
                            if where == "set":
                                src, sig = PS[:, o + c:o + c + m], free[place.bank_set()]
                            else:
                                g = (6 + place.n["group"] % 2) * 512
                                wait_apart(dve, memset_ok, 4, [(g_full, place.at("group", 1)),
                                                               (free[place.bank_set()], place.set_count(2))])
                                src, sig = PS[:, g:g + m], g_free
                                place.add("group")
                            half_max = st["kind"] == "fox_s" and j == 0
                            acc = NM1[:] if half_max else NM[:, s % 3, heads:heads + 1]
                            ins = dve.tensor_tensor_reduce(PR[:, s % 3, p:p + m], src, bias, -st["scale"], start[:],
                                                           ALU.add, ALU.min, acc)
                            heads += not half_max
                            if half_max or j == len(st["pieces"]) - 1:
                                ins.then_inc(sig, 1)
                        place.add("use")
                    if 1 <= s < n + 1:
                        st, k = steps[s - 1], (s - 1) % 3
                        dve.wait_ge(e_ready, place.at("step", s))
                        h = st["heads"]
                        if st["pieces"][0][6] is not None:
                            wait_own(dve, dve.tensor_tensor(SM[:, k, 0:h], SM[:, k, 0:h], ES[:, k, 0:h], ALU.add))
                        wait_own(dve, dve.reciprocal(RC[:, k, 0:h], SM[:, k, 0:h]))
                        for j, (a, b) in enumerate(step_areas(st)):
                            ins = dve.tensor_scalar(PR[:, k, a:b], PR[:, k, a:b], RC[:, k, j:j + 1], None, ALU.mult)
                        ins.then_inc(p_ready, 1)
                    if 2 <= s < n + 2:
                        for tiles in steps[s - 2]["groups"]:
                            slot = ring[0] % 3
                            group_lo(dve, group_areas(tiles), PTL[:, slot, :], PTH[:, slot, :])
                            ring[0] += 1
                    if s >= 3:
                        o = (2 + 3 * ((s - 3) % 2)) * 512
                        lo(dve, [(G0L[g:g + rows, r, t:t + m], PS[p:p + rows, o + c:o + c + m], G0H[g:g + rows, r, t:t + m])
                                 for p, rows, c, g, t, m in steps[s - 3]["outs"]]).then_inc(o_free, 1)
                place.add("step", n)
                ring[0] = 0

            ring = [0]

            def down(dve, with_squares):
                wait_all_read(dve, place)
                for m in range(KT):
                    wait_full(dve, place)
                    for src, a, b in parts(place.bank_set()):
                        x = like(XT[:, m, :], a, b)
                        ins = dve.tensor_tensor(x, src, x, ALU.add)
                    ins.then_inc(free[place.bank_set()], 1)
                    place.add("use")
                    if with_squares and m >= 2:
                        add_square(dve, m - 1)
                if with_squares:
                    add_square(dve, KT - 1)
                    split_sums(dve, T)

            def rotate(dve, out):
                dve.wait_ge(trig_in, place.at("layer", 32, 32))
                place.add("rope")
                dve.wait_ge(rope_ready, place.at("rope"))
                for src, a, b in parts(place.bank_set()):
                    ins = dve.tensor_tensor(like(PR[:, 1, :], a, b), src, like(XR[:, 0, :], a, b), ALU.mult)
                ins.then_inc(free[place.bank_set()], 1)
                wait_own(dve, dve.tensor_tensor(PR[:, 0, :], PR[:, 0, :], XR[:, 1, :], ALU.mult))
                wait_read(dve, place)
                place.add("use")
                dve.tensor_tensor(out, PR[:, 0, :], PR[:, 1, :], ALU.add).then_inc(roped, 1)

            for m in range(1, KT):
                add_square(dve0, m, MEM)
            split_sums(dve0, MEM)
            inverse(dve0, RM, MEM)
            for m in range(1, KT):
                add_square(dve0, m)
            split_sums(dve0, T)

            def layer(dve, l):
                inverse(dve, PR[:, 0, :], T)
                dve.wait_ge(lc_in, place.at("layer", 32, 32))
                normalised(dve, lambda kt: XT[:, kt, :], LC[:, C_MIX:C_MIX + KT], PR[:, 0, :],
                           lambda kt: PR[:, 1 + kt % 2, :], HH, HL)
                dve.tensor_scalar(NSK[:], LC[:, C_SINK:C_STATE], -1.0, None, ALU.mult)

                dve.wait_ge(ln_done, place.at("layer", 1))
                place.add("use")
                dve.scalar_tensor_tensor(FL[:], FZ[:], 0.0, FA[:], ALU.min, ALU.subtract).then_inc(lf_ready, 1)
                dve.wait_ge(lf_ready, place.at("layer", 1))
                dve.wait_ge(h_ready, place.at("ntile"))
                dve.tensor_tensor_scan(C8[:, 0:SEQ], one[0:8, :].to_broadcast([8, SEQ]), FL[:, 0:SEQ], 0.0, ALU.mult, ALU.add)
                wait_own(dve, dve.tensor_tensor_scan(C8[:, SEQ:SEQ + PAST], one[0:8, :].to_broadcast([8, PAST]), CLF[:], 0.0,
                                                     ALU.mult, ALU.add))
                wait_own(dve, dve.tensor_tensor_scan(C8[:, SEQ + PAST:N_C8], one[0:8, :].to_broadcast([8, DEC]), FL[:, SEQ:T],
                                                     C8[:, SEQ + PAST - 1:SEQ + PAST], ALU.mult, ALU.add))
                dve.tensor_scalar(C8[:], C8[:], -1.0 / FOX_SCALE, None, ALU.mult).then_inc(c_ready, 1)

                def fox(dve, turn):
                    for half in range(2):
                        lo_tile(dve, QL, QH)
                        lo_tile(dve, KL, KH)
                        place.add("use")
                        value_groups(dve, V_GROUPS, lambda t: 128 if t < NB else DEC)
                        sample_queries(dve)
                        attention(dve, fox_steps(), half)
                    down(dve, False)

                repeat(dve, place, 2, fox)

                rotate(dve, XR[:, 2, :])
                place.add("use")
                value_groups(dve, V_GROUPS, lambda t: 128 if t < NB else DEC)
                for pair in range(PAIRS):
                    rotate(dve, PR[:, 2, :])
                    dve.wait_ge(roped, place.at("rope"))
                    if pair % 2 == 0:
                        lo(dve, [(KL[:], T32[:], KH[:])])
                    wait_own(dve, lo(dve, [(QL[:], PR[:, 2, :], QH[:])]))
                    sample_queries(dve)
                    attention(dve, swa_steps(pair), pair % 2)
                    if pair == PAIRS - 1:
                        dve.wait_ge(mem_in, place.at("layer", 32, 16))
                        normalised(dve, lambda kt: MR[:, kt, :], LC[:, C_TOK:C_TOK + KT], RM[:],
                                   lambda kt: MT[:, kt % 2, :], MH, ML)
                    if pair % 2:
                        down(dve, pair == PAIRS - 1)

                for m in range(2 * MEM_H):
                    h = m % MEM_H
                    if m < MEM_H:
                        o = place.bank_set() * 1536
                        c = slice(h * MEM, (h + 1) * MEM)
                        lo(dve, [(KL[:, c], PS[:, o:o + MEM], KH[:, c])]).then_inc(free[place.bank_set()], 1)
                        place.add("use")
                    else:
                        place.add("use")
                        value_groups(dve, [[0, 1]], lambda t: 128, first=2 * h)
                inverse(dve, PR[:, 0, :], T)
                normalised(dve, lambda kt: XT[:, kt, :], LC[:, C_MEM:C_MEM + KT], PR[:, 0, :],
                           lambda kt: PR[:, 1 + kt % 2, :], HH, HL)
                for head in range(MEM_H):
                    lo_tile(dve, QL, QH)
                    sample_queries(dve)
                    attention(dve, mem_steps(head), head % 2)
                    if head % 2:
                        down(dve, head == MEM_H - 1)
                inverse(dve, PR[:, 0, :], T)
                normalised(dve, lambda kt: XT[:, kt, :], LC[:, C_FFN:C_FFN + KT], PR[:, 0, :],
                           lambda kt: PR[:, 1 + kt % 2, :], HH, HL)
                for r in range(2):
                    ins = dve.memset(GP[:, r, 0:2], 0.0)
                wait_own(dve, ins)

                def gates(dve, f, g):
                    for r in range(2):
                        dve.wait_ge(gate_ready, place.at("glu", r + 1))
                        w = [LC[:, ds((f + r) * 3 + (C_CONV + j), 1)] for j in range(3)]
                        y = YY[:, r, 0:T + 2]
                        wait_own(dve, dve.tensor_scalar(y, GP[:, r, 0:T + 2], w[0], LC[:, ds((f + r) + C_BCONV, 1)],
                                                        ALU.mult, ALU.add))
                        wait_own(dve, dve.scalar_tensor_tensor(y, GP[:, r, 1:T + 3], w[1], y, ALU.mult, ALU.add))
                        dve.scalar_tensor_tensor(y, GP[:, r, 2:T + 4], w[2], y, ALU.mult, ALU.add).then_inc(conv_done, 1)
                        place.add("use")
                        s = place.bank_set()
                        b = s * 1536 + 1024
                        wait_full(dve, place)
                        dve.wait_ge(silu_done, place.at("glu", r + 1))
                        two, _, _ = parts(s)[0]
                        y2 = YY[:, r, 0:768].rearrange("p (c n) -> p c n", c=2)
                        dve.tensor_tensor(y2, two, y2, ALU.mult)
                        y3, y4 = YY[:, r, 768:SEQ], YY[:, r, SEQ + 2:T + 2]
                        dve.tensor_tensor(y3, PS[:, b:b + SEQ - 768], y3, ALU.mult)
                        dve.tensor_tensor(y4, PS[:, b + SEQ - 768:b + T - 768], y4, ALU.mult).then_inc(free[s], 1)
                        place.add("use")
                        lo(dve, [(GL[g][:, r, 0:SEQ], YY[:, r, 0:SEQ], GH[g][:, r, 0:SEQ]),
                                 (GL[g][:, r, SEQ:T], YY[:, r, SEQ + 2:T + 2], GH[g][:, r, SEQ:T])]).then_inc(glu_ready, 1)
                    place.add("glu", 2)

                gates(dve, 0, 0)

                def mixer(dve, turn):
                    for b in range(2):
                        gates(dve, turn * 4 + 2 * (b + 1), 1 - b)
                        down(dve, False)

                repeat(dve, place, (FT // 2 - 1) // 2, mixer)
                down(dve, True)
                place.add("layer")

            repeat(dve0, place, DEPTH, layer)
            inverse(dve0, PR[:, 0, :], T)
            for kt in range(KT):
                dve0.scalar_tensor_tensor(YT[:, kt, :], XT[:, kt, :], FC[:, kt:kt + 1], PR[:, 0, :], ALU.mult, ALU.mult)\
                    .then_inc(y_ready, 1)


def _in_blocks(w):
    return w.reshape(2, 4, 128, 128).transpose(0, 2, 1, 3).reshape(2, 128, HALF)


def _out_blocks(w2):
    return w2.reshape(2, 128, 2, HALF).transpose(2, 0, 1, 3).reshape(4, 128, HALF)


def _layer_slabs(x, l):
    w_in = x["w_in"][l]
    fox = FOX_H * HD
    f0, s0 = 3 * fox, 3 * fox + FOX_H
    k0, v0 = s0 + SWA_H * HD, s0 + SWA_H * HD + SWA_KV * HD
    out = [_in_blocks(np.tile(w_in[:, f0:s0], (1, 16)))]
    w_out = x["w_out"][l].reshape(8, 128, D)
    ck, cv = x["cache_fox_k"][l, 0], x["cache_fox_v"][l, 0]
    for p in range(PAIRS):
        for a in (0, fox, 2 * fox):
            out.append(_in_blocks(w_in[:, a + p * 128:a + (p + 1) * 128]))
        kp = ck[:, 2 * p:2 * p + 2].reshape(PAST, 128)
        vp = cv[:, 2 * p:2 * p + 2].reshape(PAST, 128)
        out.append(kp.T.reshape(128, 2, HALF).transpose(1, 0, 2))
        out.append(vp.reshape(2, 4, 128, 128).transpose(0, 2, 1, 3).reshape(2, 128, HALF))
        if p % 2:
            out.append(_out_blocks(w_out[p - 1:p + 1]))
    out.append(_in_blocks(w_in[:, k0:v0]))
    out.append(_in_blocks(w_in[:, v0:v0 + 128]))
    sk, sv = x["cache_swa_k"][l, 0], x["cache_swa_v"][l, 0]
    for p in range(PAIRS):
        out.append(_in_blocks(w_in[:, s0 + p * 128:s0 + (p + 1) * 128]))
        kt = sk[:, p // 2].T
        out.append(np.concatenate([np.concatenate([kt, kt]), sv.reshape(KEEP, 128), np.zeros((128, 256), np.float32)], 1)[None])
        if p % 2:
            out.append(_out_blocks(w_out[PAIRS + p - 1:PAIRS + p + 1]))
    for w in (x["w_mk"][l], x["w_mv"][l]):
        for m in range(MEM_H):
            out.append(_in_blocks(w[:, m * 128:(m + 1) * 128]))
    w_mo = x["w_mo"][l].reshape(MEM_H, 128, D)
    for m in range(MEM_H):
        out.append(_in_blocks(x["w_mq"][l][:, m * 128:(m + 1) * 128]))
        mk, mv = x["cache_mem_k"][l, 0, :, m], x["cache_mem_v"][l, 0, :, m]
        out.append(np.concatenate([mk.T, mv.reshape(2, 128, 128).transpose(1, 0, 2).reshape(128, 256)], 1)[None])
        if m % 2:
            out.append(_out_blocks(w_mo[m - 1:m + 1]))
    w_up, w_down = x["w_up"][l], x["w_down"][l].reshape(FT, 128, D)

    def up(g):
        for f in (2 * g, 2 * g + 1):
            out.append(_in_blocks(w_up[:, f * 128:(f + 1) * 128]))
            out.append(_in_blocks(w_up[:, FF + f * 128:FF + (f + 1) * 128]))

    up(0)
    for g in range(1, FT // 2):
        up(g)
        out.append(_out_blocks(w_down[2 * g - 2:2 * g]))
    out.append(_out_blocks(w_down[FT - 2:FT]))
    out.append(np.zeros((2, 128, HALF), np.float32))
    out = np.concatenate(out)
    assert out.shape == (N_SLABS, 128, HALF), out.shape
    return out


def _layer_constants(x, l):
    def columns(v):
        return v.reshape(-1, 128).T

    c = [columns(x[n][l]) for n in ("ln_mix", "ln_mem", "ln_memtok", "ln_ffn")]
    c.append(x["w_conv"][l].reshape(3, FT, 128).transpose(2, 1, 0).reshape(128, 3 * FT))
    c.append(columns(x["b_conv"][l]))
    c.append(np.tile(x["b_f"][l], 16)[:, None])
    sinks = x["swa_sinks"][l]
    c.append(np.broadcast_to(sinks, (128, SWA_H)))
    c.append(np.repeat(sinks.reshape(PAIRS, 2).T, 64, axis=0))
    c.append(x["state_conv"][l, 0].reshape(2, FT, 128).transpose(2, 1, 0).reshape(128, 2 * FT))
    return np.concatenate(c, 1)


_OUTS = [("y", (128, KT, T)), ("fk", (DEPTH * PAIRS, 128, T)), ("fv", (DEPTH * PAIRS, 128, T)),
         ("lf", (DEPTH, 8, T)), ("sk", (DEPTH, 128, KEEP + DEC)), ("sv", (DEPTH, 128, KEEP + DEC)),
         ("mk", (DEPTH * MEM_H, 128, MEM)), ("mv", (DEPTH * MEM_H, 128, MEM)), ("cv", (DEPTH, 128, FT * 4)),
         ("tk", (DEPTH, KEEP - DEC, 128)), ("tv", (DEPTH, KEEP - DEC, 128))]


def kernel(**inputs):
    import concourse.bacc as _bacc
    from concourse import mybir as _mybir
    from concourse.bass_utils import run_bass_kernel_spmd as _run

    x = {n: np.asarray(v) for n, v in inputs.items()}
    tokens = np.concatenate([x["x_prompt"][0], x["x_sample"][0]])

    def feature_major(v):
        return v.T.reshape(KT, 128, -1).transpose(1, 0, 2)

    data = {
        "xT": feature_major(tokens),
        "memT": feature_major(x["mem_prompt"][0]),
        "slabs": np.concatenate([_layer_slabs(x, l) for l in range(DEPTH)]),
        "layer_c": np.stack([_layer_constants(x, l) for l in range(DEPTH)]),
        "final_c": x["ln_final"].reshape(KT, 128).T,
        "clogf": x["cache_fox_logf"][:, 0].transpose(0, 2, 1),
        "swa_tail_k": x["cache_swa_k"][:, 0, DEC:].reshape(DEPTH, KEEP - DEC, 128),
        "swa_tail_v": x["cache_swa_v"][:, 0, DEC:].reshape(DEPTH, KEEP - DEC, 128),
    }
    nc = _bacc.Bacc("TRN2", target_bir_lowering=False, num_devices=1, dynamic_dma_scratch_size=1024)
    arrays, args = {}, []
    for name, a in data.items():
        a = np.ascontiguousarray(a)
        arrays[f"in_{name}"] = a
        args.append(nc.dram_tensor(f"in_{name}", a.shape, _mybir.dt.from_np(a.dtype), kind="ExternalInput").ap())
    for name, shape in _OUTS:
        args.append(nc.dram_tensor(f"out_{name}", shape, _mybir.dt.float32, kind="ExternalOutput").ap())
    encoder_step(nc, *args)
    r = _run(nc, [arrays], core_ids=[0]).results[0]
    got = {name: r[f"out_{name}"] for name, _ in _OUTS}

    def heads(a, n, hd, tokens):
        a = a.reshape(DEPTH, n * hd, -1).transpose(0, 2, 1)[:, tokens]
        return a.reshape(DEPTH, 1, a.shape[1], n, hd)

    prompt, sample = slice(0, SEQ), slice(SEQ, T)
    y = got["y"].transpose(2, 1, 0).reshape(T, D)
    lf = got["lf"].transpose(0, 2, 1)
    cv = got["cv"].reshape(DEPTH, 128, FT, 2, 2).transpose(3, 0, 4, 2, 1).reshape(2, DEPTH, 1, 2, FF)

    def window(tail, own):
        a = np.concatenate([tail, own.transpose(0, 2, 1)[:, KEEP:]], 1)
        return a.reshape(DEPTH, 1, KEEP, SWA_KV, HD)

    return (y[None, prompt], y[None, sample],
            heads(got["fk"], FOX_H, HD, prompt), heads(got["fv"], FOX_H, HD, prompt), lf[:, None, prompt],
            heads(got["sk"], SWA_KV, HD, slice(0, KEEP)), heads(got["sv"], SWA_KV, HD, slice(0, KEEP)),
            heads(got["mk"], MEM_H, 128, slice(0, MEM)), heads(got["mv"], MEM_H, 128, slice(0, MEM)), cv[0],
            heads(got["fk"], FOX_H, HD, sample), heads(got["fv"], FOX_H, HD, sample), lf[:, None, sample],
            window(got["tk"], got["sk"]), window(got["tv"], got["sv"]), cv[1])
```

```python
from contextlib import ExitStack, contextmanager

import numpy as np

import concourse.bass as bass
from concourse import mybir

F32 = mybir.dt.float32
F32R = mybir.dt.float32r
ACT = mybir.ActivationFunctionType
ALU = mybir.AluOpType
ds = bass.ds

DEPTH, D, SEQ, DEC, PAST = 2, 1024, 1024, 64, 1024
T = SEQ + DEC
KT = D // 128
FOX_H, HD = 8, 64
SWA_H, SWA_KV = 8, 2
PAIRS = FOX_H // 2
MEM, MEM_H = 256, 4
FF = 2816
FT = FF // 128
NB = SEQ // 128
KEEP = 128
EPS = 1e-6
NEG = -1e30
CH = [(0, 384), (384, 768), (768, T)]
HALF = 512
STAT_AT = 2
MEM_TILES = -(-KT * MEM // T)
THIRD, OUTS = 5 * 512, 4 * 512
FOX_SLABS = 10
N_SLABS = 2 + PAIRS * FOX_SLABS + 8 + (4 + PAIRS * 3) + 8 + 16 + MEM_H * 3 + 8 + FT * 6 + 2
assert N_SLABS % 4 == 0
C_MIX, C_MEM, C_TOK, C_FFN = 0, 8, 16, 24
C_CONV = 32
C_BCONV = C_CONV + 3 * FT
C_BF = C_BCONV + FT
C_SINK = C_BF + 1
C_SINK2 = C_SINK + SWA_H
C_STATE = C_SINK2 + PAIRS
N_LC = C_STATE + 2 * FT
N_C8 = SEQ + PAST + DEC


class Place:

    KINDS = ("layer", "slab", "use", "group", "ring", "step", "hi", "self", "store", "norm", "bias", "glu",
             "ntile", "rope", "attn", "third")

    def __init__(self):
        self.n = dict.fromkeys(self.KINDS, 0)
        self.loops = []

    def at(self, kind, more=0, scale=1):
        value = self.n[kind] * scale + more
        for turn, per in self.loops:
            if per[kind]:
                value = turn * (per[kind] * scale) + value
        return value

    def bank_set(self):
        return self.n["use"] % 2

    def set_count(self, more=0):
        value = self.n["use"] // 2 + more
        for turn, per in self.loops:
            if per["use"]:
                value = turn * (per["use"] // 2) + value
        return value

    def uses_of(self, s, more=0):
        value = (self.n["use"] + 1 - s) // 2 + more
        for turn, per in self.loops:
            if per["use"]:
                value = turn * (per["use"] // 2) + value
        return value

    def add(self, kind, k=1):
        self.n[kind] += k


class Silent:

    def __getattr__(self, name):
        return lambda *a, **k: self

    @contextmanager
    def Fori(self, a, b):
        yield 0


def repeat(eng, place, turns, body):
    before = dict(place.n)
    body(Silent(), 0)
    per = {k: place.n[k] - before[k] for k in before}
    assert per["use"] % 2 == 0 and per["group"] % 2 == 0 and per["slab"] % 4 == 0, per
    place.n = dict(before)
    with eng.Fori(0, turns) as turn:
        place.loops.append((turn, per))
        body(eng, turn)
        place.loops.pop()
    place.n = {k: before[k] + turns * per[k] for k in before}


def wait_apart(eng, constant, value, waits):
    held = [(s, v if isinstance(v, int) else eng.to_reg(v)) for s, v in waits]
    eng.wait_ge(constant, value)
    for s, v in held:
        eng.wait_ge(s, v)
    for _, v in held:
        if not isinstance(v, int) and not isinstance(eng, Silent):
            eng.free_register(v)


def encoder_step(nc, xT, memT, slabs, layer_c, final_c, clogf, swa_tail_k, swa_tail_v,
                 o_y, o_fk, o_fv, o_lf, o_sk, o_sv, o_mk, o_mv, o_cv, o_tk, o_tv):
    ctx = ExitStack()
    with ctx:
        def sem(name):
            return ctx.enter_context(nc.semaphore(name))

        at = [(nc.sbuf_base + 31) // 32 * 32]

        def here(name, shape, dt, offset):
            return nc.alloc_sbuf_tensor_at(name, shape, dt, offset=offset)

        def sb(name, shape, dt=F32):
            size = 4 * int(np.prod(shape[1:]))
            offset = at[0]
            at[0] = offset + (size + 31) // 32 * 32
            return here(name, shape, dt, offset)

        XT = sb("XT", [128, KT, T])
        HH0 = at[0]
        HH, HL = (sb(n, [128, KT, T], F32R) for n in ("HH", "HL"))
        RAW = sb("RAW", [128, 4, HALF])
        WH, WL = (sb(n, [128, 4, HALF], F32R) for n in ("WH", "WL"))
        G0H, G0L = (sb(n, [128, 2, T], F32R) for n in ("G0H", "G0L"))
        ident = sb("ident", [128, 128])
        ident_r = sb("ident_r", [128, 128], F32R)
        mean_r = sb("mean_r", [128, 128], F32R)
        causal = sb("causal", [128, 128])
        causal_r = sb("causal_r", [128, 128], F32R)
        tail_mask = sb("tail_mask", [128, DEC])
        tail_mask_r = sb("tail_mask_r", [128, DEC], F32R)
        band = sb("band", [128, 256])
        zero = sb("zero", [128, 256])
        big = sb("big", [128, 1])
        eps = sb("eps", [128, 1])
        one = sb("one", [128, 1])
        LC = sb("LC", [128, N_LC])
        FC = sb("FC", [128, KT])
        NSK = sb("NSK", [128, SWA_H + PAIRS])
        RM = sb("RM", [128, MEM])
        CO = sb("CO", [128, FT * 4])
        NM = sb("NM", [128, 3, 2])
        NM1 = sb("NM1", [128, 1])
        SM = sb("SM", [128, 3, 2])
        ES = sb("ES", [128, 3, 2])
        RC = sb("RC", [128, 3, 2])
        QSH, QSL = (sb(n, [128, 128], F32R) for n in ("QSH", "QSL"))
        U0 = at[0]
        QH, QL = (sb(n, [128, T], F32R) for n in ("QH", "QL"))
        KH0, VH0 = at[0], at[0] + 2 * 4 * T
        KH, KL = (sb(n, [128, T], F32R) for n in ("KH", "KL"))
        VH, VL = (sb(n, [128, 9 * 128], F32R) for n in ("VH", "VL"))
        T32 = sb("T32", [128, T])
        XR0 = at[0]
        XR = sb("XR", [128, 3, T])
        PR0 = at[0]
        PR = sb("PR", [128, 3, T])
        PT0 = at[0]
        PTH, PTL = (sb(n, [128, 3, 512], F32R) for n in ("PTH", "PTL"))
        assert at[0] <= nc.sbuf_top, (at[0], nc.sbuf_top)
        ACC = here("ACC", [128, T], F32, XR0 + 4 * KT * MEM)
        SQ = [here(f"SQ{i}", [128, T], F32, U0 + 4 * T * i) for i in range(2)]
        SH, SL = QH, QL
        assert XR0 + 4 * KT * MEM + 4 * T <= PR0
        FZ = here("FZ", [8, T], F32, KH0)
        FA = here("FA", [8, T], F32, KH0 + 4 * T)
        FL = here("FL", [8, T], F32, VH0)
        CLF = here("CLF", [8, PAST], F32, VH0 + 4 * 1152)
        C8 = here("C8", [8, N_C8], F32, PR0)
        MR = here("MR", [128, KT, MEM], F32, XR0)
        MEM_AT = 4 * T * (KT - MEM_TILES)
        MH = here("MH", [128, KT, MEM], F32R, HH0 + MEM_AT)
        ML = here("ML", [128, KT, MEM], F32R, HH0 + 4 * T * KT + MEM_AT)
        PW = here("PW", [128, 3, 512], F32, PR0)
        RX = here("RX", [128, T], F32, PR0 + 4 * 1536)
        MT = here("MT", [128, 2, MEM], F32, PR0 + 4 * 1536)
        QX = here("QX", [128, T], F32, U0 + 4 * T)
        MQH, MQL = (here(n, [128, T], F32R, XR0 + 4 * T * i) for i, n in enumerate(("MQH", "MQL")))
        QUERIES = [(QH, QL), (MQH, MQL)]
        G1H, G1L = (here(n, [128, 2, T], F32R, U0 + i * 8 * T) for i, n in enumerate(("G1H", "G1L")))
        GP = here("GP", [128, 2, T + 4], F32, U0 + 16 * T)
        YY = here("YY", [128, 2, T + 4], F32, U0 + 16 * T + 8 * (T + 4))
        assert U0 + 16 * T + 16 * (T + 4) <= PR0
        YT = here("YT", [128, KT, T], F32, HH0)
        GH, GL = [G0H, G1H], [G0L, G1L]
        PS = ctx.enter_context(nc.psum_tensor("PS", [128, 8 * 512], F32))
        decays = nc.dram_tensor("decays", [8, N_C8], F32).ap()

        half_hd = HD // 2
        inv = (np.float32(10000.0) ** (-np.arange(half_hd, dtype=np.float32) / np.float32(half_hd))).astype(np.float32)
        angle = (np.arange(T, dtype=np.float32)[:, None] * inv[None, :]).astype(np.float32).T.astype(np.float64)
        cos_t = nc.inline_tensor(np.tile(np.cos(angle), (4, 1)).astype(np.float32), name="cos_t").ap()
        sin_t = nc.inline_tensor(np.concatenate([-np.sin(angle), np.sin(angle)] * 2).astype(np.float32), name="sin_t").ap()
        q, k = np.arange(128)[:, None], np.arange(256)[None, :]
        c_ident = nc.inline_tensor(np.eye(128, dtype=np.float32), name="c_ident").ap()
        c_causal = nc.inline_tensor(np.where(k[:, :128] > q, NEG, 0).astype(np.float32), name="c_causal").ap()
        c_tail = nc.inline_tensor(np.where(k[:, :DEC] > q % DEC, NEG, 0).astype(np.float32), name="c_tail").ap()
        seen = np.where(q < 64, k < 192, k >= 64)
        c_band = nc.inline_tensor(np.where(seen, 0, NEG).astype(np.float32), name="c_band").ap()

        x_in = [sem(f"x_in{i}") for i in range(KT)]
        const_in, mem_in, const_ok, memset_ok = sem("const_in"), sem("mem_in"), sem("const_ok"), sem("memset_ok")
        raw_in = [sem(f"raw_in{i}") for i in range(4)]
        w_hi, w_ready, w_used = sem("w_hi"), sem("w_ready"), sem("w_used")
        full = [sem("full0"), sem("full1")]
        free = [sem("free0"), sem("free1")]
        third_free = sem("third_free")
        g_full, g_free = sem("g_full"), sem("g_free")
        hi_done = sem("hi_done")
        act_self, dve_self = sem("act_self"), sem("dve_self")
        e_ready = sem("e_ready")
        p_ready = sem("p_ready")
        p_used = sem("p_used")
        pt_used = sem("pt_used")
        o_full, o_free = sem("o_full"), sem("o_free")
        t32_out = sem("t32_out")
        sq_ready, sq_used = sem("sq_ready"), sem("sq_used")
        stat_ready, rms_ready, attn_ready = sem("stat_ready"), sem("rms_ready"), sem("attn_ready")
        ht_ready, h_ready = sem("ht_ready"), sem("h_ready")
        lc_in, ln_done, lf_ready, c_ready, c_stored, lf_out = (sem(n) for n in ("lc_in", "ln_done", "lf_ready", "c_ready", "c_stored", "lf_out"))
        bias_in, trig_in, swap_in, roped = sem("bias_in"), sem("trig_in"), sem("swap_in"), sem("roped")
        gate_ready, conv_done, silu_done, glu_ready = sem("gate_ready"), sem("conv_done"), sem("silu_done"), sem("glu_ready")
        co_out = sem("co_out")
        out_done = sem("out_done")
        k32_out = sem("k32_out")
        y_ready = sem("y_ready")

        block = ctx.enter_context(nc.Block())

        def bank(i):
            return PS[:, i * 512:(i + 1) * 512]

        def parts(s):
            two = PS[:, s * 1024:(s + 1) * 1024].rearrange("p (c n) -> p c n", c=2)[:, :, 0:384]
            return [(PS[:, THIRD:THIRD + T - 768], 768, T), (two, 0, 768)]

        def over_tile(place, op, last_reader=False):
            s = place.bank_set()
            for src, a, b in parts(s):
                ins = op(src, a, b)
                if last_reader:
                    ins.then_inc(third_free if a == 768 else free[s], 1)
            return ins

        def probs(st, k, a, b):
            return PW[:, k, a:b] if st["kind"] in ("swa", "swa_s") else PR[:, k, a:b]

        def like(ap, a, b):
            return ap[:, a:b].rearrange("p (c n) -> p c n", c=2) if b - a == 768 else ap[:, a:b]

        FOX_SCALE = float(HD) ** -0.5
        MEM_SCALE = float(128) ** -0.5

        def both(n, first):
            plan = []
            for j in range(n):
                plan += [(first + j, 256, 0, j == 0, j == n - 1), None]
            return plan

        def fox_steps():
            steps = []
            order = []
            blocks = [[7], [0, 1], [6], [2, 3], [5], [4]]
            for h in range(2):
                order += [(1 - h if k % 2 else h, b) for k, b in enumerate(blocks)]
            for h, b in order:
                widths = [(i + 1) * 128 for i in b]
                starts = [0, widths[0]][:len(b)]
                joint = b[0] + 1
                tiles = [(p + j * 128, 128) for j in range(joint) for p in starts]
                plan = []
                for j in range(joint):
                    plan += [(j, 128 * len(b), 0, j == 0, j == joint - 1 and len(b) == 1)] + [None] * (len(b) - 1)
                if len(b) == 2:
                    tiles.append((starts[1] + joint * 128, 128))
                    plan.append((joint, 128, 128, False, True))
                steps.append(dict(kind="fox", h=h, blocks=b, width=sum(widths), heads=len(b),
                                  pieces=[("set", 512 * k, starts[k], n, XR[:, h, 0:n], big, None)
                                          for k, n in enumerate(widths)],
                                  groups=[tiles[a:a + 4] for a in range(0, len(tiles), 4)], plan=plan,
                                  outs=[(64 * h, 64, 0, 64 * h, b[0] * 128, 128 * len(b))], scale=FOX_SCALE))
            tiles = [(j * 128, 128) for j in range(PAST // 128)]
            steps.insert(0, dict(kind="fox_s", width=PAST + DEC, heads=1,
                              pieces=[("set", 0, 0, PAST, XR[:, 2, 0:PAST], big, None),
                                      ("group", 0, PAST, DEC, XR[:, 2, PAST:T], NM1, None)],
                              groups=[tiles[0:4], tiles[4:8], [(PAST, DEC)]],
                              outs=[(64 * h, 64, 64 * h, 64 * h, SEQ, DEC) for h in range(2)], scale=FOX_SCALE))
            return steps

        def swa_steps(pair):
            steps = []
            kv = 64 * (pair // 2)
            for i in range(NB):
                n = 128 if i == 0 else 256
                steps.append(dict(kind="swa", i=i, pair=pair, width=512, heads=2,
                                  pieces=[("set", 512 * h, 256 * h, n, band[:, 256 - n:256],
                                           NSK[:, 2 * pair + h:2 * pair + h + 1], 2 * pair + h) for h in range(2)],
                                  groups=[[(256 * h + 128 * j, 128) for j in range(n // 128) for h in range(2)]],
                                  plan=both(n // 128, max(0, i - 1)),
                                  outs=[(kv, 64, 128 * h, 64 * h, i * 128, 128) for h in range(2)], scale=FOX_SCALE))
            steps.insert(0, dict(kind="swa_s", pair=pair, width=KEEP + DEC, heads=1,
                              pieces=[("set", 0, 0, KEEP + DEC, zero[:, 0:KEEP + DEC],
                                       NSK[:, SWA_H + pair:SWA_H + pair + 1], SWA_H + pair)],
                              groups=[[(0, 128), (128, DEC)]],
                              outs=[(kv, 64, 64 * h, 64 * h, SEQ, DEC) for h in range(2)], scale=FOX_SCALE))
            return steps

        def mem_steps(head):
            steps = [dict(kind="mem", i=i, head=head, width=2 * MEM, heads=2,
                          pieces=[("set", 512 * h, MEM * h, MEM, zero[:, 0:MEM], big, None) for h in range(2)],
                          groups=[[(MEM * h + 128 * j, 128) for j in range(MEM // 128) for h in range(2)]],
                          plan=both(MEM // 128, head * 2),
                          outs=[(0, 128, 0, 0, i * 256, 256)], scale=MEM_SCALE) for i in range(NB // 2)]
            steps.insert(0, dict(kind="mem_s", head=head, width=MEM, heads=1,
                              pieces=[("set", 0, 0, MEM, zero[:, 0:MEM], big, None)],
                              groups=[[(0, 128), (128, 128)]],
                              outs=[(0, 128, 0, 0, SEQ, DEC)], scale=MEM_SCALE))
            return steps

        V_GROUPS = [[0, 1, 2], [3, 4], [5, 6], [7, 8]]

        def group_areas(tiles):
            whole = [j for j, (_, rows) in enumerate(tiles) if rows == 128]
            areas = [(128, 0, 128 * len(whole))] if whole else []
            return areas + [(rows, 128 * j, 128) for j, (_, rows) in enumerate(tiles) if rows < 128]

        @block.sync
        def _(sp):
            for a, b in ((ident, c_ident), (causal, c_causal), (tail_mask, c_tail), (band, c_band), (FC, final_c)):
                sp.dma_start(a[:], b).then_inc(const_in, 16)
            sp.dma_start(MR[:, :, :], memT).then_inc(mem_in, 16)
            for kt in range(KT):
                sp.dma_start(XT[:, kt, :], xT[:, kt, :]).then_inc(x_in[kt], 16)
            for s in range(4):
                sp.dma_start(RAW[:, s, :], slabs[s]).then_inc(raw_in[s], 16)
            with sp.Fori(1, DEPTH * N_SLABS // 4) as turn:
                for s in range(4):
                    sp.wait_ge(w_ready, turn * 4 + (s - 3))
                    sp.dma_start(RAW[:, s, :], slabs[ds(turn * 4 + s, 1)].rearrange("o p n -> p (o n)")).then_inc(raw_in[s], 16)
            for l in range(DEPTH):
                sp.dma_start(o_tk[l], swa_tail_k[l]).then_inc(out_done, 16)
                sp.dma_start(o_tv[l], swa_tail_v[l]).then_inc(out_done, 16)
            sp.wait_ge(out_done, 16 * (2 * DEPTH + KT))
            sp.wait_ge(lf_out, 16 * DEPTH)
            sp.wait_ge(k32_out, 16 * DEPTH)
            sp.wait_ge(t32_out, 16 + 16 * DEPTH * (2 * PAIRS + 1 + 2 * MEM_H))
            sp.wait_ge(co_out, 16 + 16 * DEPTH)

        @block.gpsimd
        def _(pool):
            pool.memset(zero[:], 0.0).then_inc(memset_ok, 1)
            pool.memset(big[:], 3.0e38).then_inc(memset_ok, 1)
            pool.memset(eps[:], EPS).then_inc(memset_ok, 1)
            pool.memset(one[:], 1.0).then_inc(memset_ok, 1)

            def split(turn, s):
                pool.wait_ge(raw_in[s], turn * 16 + 16)
                if not isinstance(turn, int):
                    pool.wait_ge(w_used, turn * 4 + (s - 3))
                pool.tensor_tensor(WH[:, s, :], RAW[:, s, :], zero[:, 0:1].to_broadcast([128, HALF]), ALU.add).then_inc(w_hi, 1)
                pool.wait_ge(w_hi, turn * 4 + (s + 1))
                pool.tensor_tensor(WL[:, s, :], RAW[:, s, :], WH[:, s, :].bitcast(F32), ALU.subtract).then_inc(w_ready, 1)

            pool.wait_ge(memset_ok, 4)
            for s in range(4):
                split(0, s)
            with pool.Fori(1, DEPTH * N_SLABS // 4) as turn:
                for s in range(4):
                    split(turn, s)

        @block.tensor
        def _(pe0):
            place = Place()
            pe0.wait_ge(const_ok, 5)
            pe0.wait_ge(const_in, 80)
            pe0.sem_inc(p_used, 3)
            pe0.sem_inc(pt_used, 3)
            held_groups = []
            owed = []
            state = {"last": None, "bare": False}

            def mm(pe, *a, **k):
                ins = pe.matmul(*a, **k)
                state["last"], state["bare"] = ins, not owed
                if owed:
                    ins.then_inc(owed.pop(0), 1)

            def signal(s, now=False):
                if state["bare"]:
                    state["last"].then_inc(s, 1)
                    state["bare"] = False
                else:
                    assert not now
                    owed.append(s)

            def claim(pe):
                s = place.bank_set()
                pe.wait_ge(free[s], place.set_count(1))
                return s

            def at(s, c):
                return THIRD if c == 2 else s * 1024 + c * 512

            def products(pe, s, steps, chunks, first, last):
                for cs in ([c for c in (range(2), range(2, 3)) if c[0] < len(chunks)] if first else [range(3)]):
                    if first and cs[0] == 2:
                        pe.wait_ge(third_free, place.at("third", 1))
                        place.add("third")
                    for i, terms in enumerate(steps):
                        for k, (w, x) in enumerate(terms):
                            for c in cs:
                                if c < len(chunks):
                                    a, b = chunks[c]
                                    o = at(s, c)
                                    mm(pe, PS[:, o:o + b - a], w, x[:, a:b], start=(first and i == 0 and k == 0),
                                       stop=(last and i == len(steps) - 1 and k == len(terms) - 1))

            def done(s):
                signal(full[s], now=True)
                place.add("use")

            def slab(pe):
                slot = place.n["slab"] % 4
                pe.wait_ge(w_ready, place.at("slab", 1))
                place.add("slab")
                return slot

            def project(pe, xh, xl, chunks, fresh=None):
                s = claim(pe)
                for half in range(2):
                    slot = slab(pe)
                    for ks in ((0, 1), (2,), (3,)):
                        steps = []
                        for k in ks:
                            kt = half * 4 + k
                            if fresh is not None and k == ks[-1]:
                                pe.wait_ge(h_ready, place.at("ntile", fresh + kt + 1))
                            steps.append([(w[:, slot, k * 128:(k + 1) * 128], x[:, kt, :])
                                          for w, x in ((WH, xh), (WH, xl), (WL, xh))])
                        products(pe, s, steps, chunks, kt == 1, kt == KT - 1)
                    if half == 0:
                        signal(w_used, now=True)
                done(s)
                signal(w_used)

            def down(pe, b):
                slots = None
                for m in range(KT):
                    s = claim(pe)
                    if m % 4 == 0:
                        slots = [slab(pe), slab(pe)]
                    steps = [[(w[:, slots[r], (m % 4) * 128:(m % 4 + 1) * 128], x[:, r, :])
                              for w, x in ((WH, GH[b]), (WH, GL[b]), (WL, GH[b]))] for r in range(2)]
                    if m % 4 < 3:
                        products(pe, s, steps, CH, True, True)
                    else:
                        products(pe, s, steps[:1], CH, True, False)
                        signal(w_used, now=True)
                        products(pe, s, steps[1:], CH, False, True)
                    done(s)
                    if m % 4 == 3:
                        signal(w_used)

            def stat(pe, width):
                s = claim(pe)
                pe.wait_ge(stat_ready, place.at("norm", 1))
                products(pe, s, [[(mean_r[:], SH[:]), (mean_r[:], SL[:])]], CH if width == T else [(0, width)], True, True)
                done(s)
                place.add("norm")

            def value_tiles(pe, tiles_of, rows_of, back):
                place.add("use", -back)
                pe.wait_ge(free[place.bank_set()], place.set_count(2))
                place.add("use", back)
                for tiles in tiles_of:
                    wait_apart(pe, const_in, 80, [(g_free, place.at("group", 1))])
                    b = 6 + place.n["group"] % 2
                    for j, tile in enumerate(tiles):
                        rows = rows_of(tile)
                        mm(pe, PS[0:rows, b * 512 + j * 128:b * 512 + (j + 1) * 128],
                           T32[:, tile * 128:tile * 128 + rows], ident[:], start=True, stop=True)
                    signal(g_full, now=True)
                    place.add("group")

            def value_hook(pe, back):
                value_tiles(pe, V_GROUPS, own_values, back)
                held_groups[:] = [place.at("group", 2)] * len(held_groups)

            def scores(pe, st, held):
                s = claim(pe)
                o = s * 1024

                def product(out, width, lh, ll, rh, rl, mask=None):
                    for a, b, last in ((lh, rh, False), (lh, rl, False), (ll, rh, True)):
                        for c in range(0, width, 512):
                            e = min(width, c + 512)
                            mm(pe, PS[:, out + c:out + e], a, b[:, c:e], start=(a is lh and b is rh),
                               stop=last and not (mask is not None and e == width))
                    if mask is not None:
                        n = mask.shape[1]
                        mm(pe, PS[:, out + width - n:out + width], ident_r[:], mask[:], start=False, stop=True)

                if st["kind"] == "fox":
                    r = slice(64 * st["h"], 64 * st["h"] + 64)
                    for k, i in enumerate(st["blocks"]):
                        n, b = (i + 1) * 128, slice(i * 128, (i + 1) * 128)
                        product(o + 512 * k, n, QH[r, b], QL[r, b], KH[r, 0:n], KL[r, 0:n], causal_r)
                elif st["kind"] == "fox_s":
                    slots = [slab(pe), slab(pe)]
                    for j in range(2):
                        product(o + 512 * j, 512, QSH[:], QSL[:], WH[:, slots[j], :], WL[:, slots[j], :])
                elif st["kind"] == "swa":
                    i = st["i"]
                    a = max(0, i - 1) * 128
                    for h in range(2):
                        r = slice(64 * h, 64 * h + 64)
                        product(o + 512 * h, (i + 1) * 128 - a, QH[r, i * 128:(i + 1) * 128], QL[r, i * 128:(i + 1) * 128],
                                KH[r, a:(i + 1) * 128], KL[r, a:(i + 1) * 128])
                elif st["kind"] == "swa_s":
                    slot = slab(pe)
                    held["v"] = slot
                    product(o, KEEP, QSH[:], QSL[:], WH[:, slot, 0:KEEP], WL[:, slot, 0:KEEP])
                    product(o + KEEP, DEC, QSH[:], QSL[:], KH[:, SEQ:T], KL[:, SEQ:T])
                elif st["kind"] == "mem":
                    i, h = st["i"], st["head"]
                    qh, ql = QUERIES[h % 2]
                    for b in range(2):
                        r = slice((2 * i + b) * 128, (2 * i + b + 1) * 128)
                        product(o + 512 * b, MEM, qh[:, r], ql[:, r], KH[:, h * MEM:(h + 1) * MEM], KL[:, h * MEM:(h + 1) * MEM])
                else:
                    slot = slab(pe)
                    held["v"] = slot
                    qh, ql = QUERIES[st["head"] % 2]
                    product(o, MEM, qh[:, T - 128:T], ql[:, T - 128:T], WH[:, slot, 0:MEM], WL[:, slot, 0:MEM])
                done(s)
                if st["kind"] == "fox_s":
                    signal(w_used)
                    signal(w_used)
                    pe.wait_ge(g_free, place.at("group", 1))
                    b = (6 + place.n["group"] % 2) * 512
                    product(b, DEC, QSH[:], QSL[:], KH[:, SEQ:T], KL[:, SEQ:T], tail_mask_r)
                    signal(g_full, now=True)
                    place.add("group")

            def transposes(pe, st, s):
                pe.wait_ge(p_ready, place.at("step", s + 1))
                for tiles in st["groups"]:
                    wait_apart(pe, const_in, 80, [(g_free, place.at("group", 1))])
                    b = 6 + place.n["group"] % 2
                    for j, (col, rows) in enumerate(tiles):
                        mm(pe, PS[0:rows, b * 512 + j * 128:b * 512 + (j + 1) * 128],
                           probs(st, s % 3, col, col + rows), ident[:], start=True, stop=True)
                    signal(g_full, now=True)
                    held_groups.append(place.at("group", 3))
                    place.add("group")
                signal(p_used)

            def values(pe, st, s, ring, held):
                o = OUTS
                pe.wait_ge(o_free, place.at("step", s + 1))
                tile = 0
                n_tiles = sum(len(g) for g in st["groups"])
                for gi, tiles in enumerate(st["groups"]):
                    pe.wait_ge(g_free, held_groups[ring + gi])
                    slot = (ring + gi) % 3
                    held_slot = None
                    if st["kind"] == "fox_s" and gi < 2:
                        held_slot = slab(pe)
                    for j, (col, rows) in enumerate(tiles):
                        out, n, q0, first, last = o, 128, 0, tile == 0, tile == n_tiles - 1
                        if "plan" in st:
                            if st["plan"][tile] is None:
                                tile += 1
                                continue
                            kt, n, c, first, last = st["plan"][tile]
                            out = o + c
                            v = [x[:, kt * 128:(kt + 1) * 128] for x in (VH, VL)]
                        elif st["kind"] == "fox_s" and rows < 128:
                            v = [x[0:rows, tile * 128:(tile + 1) * 128] for x in (VH, VL)]
                        elif st["kind"] == "fox_s":
                            v = [x[:, held_slot, j * 128:(j + 1) * 128] for x in (WH, WL)]
                        elif st["kind"] == "swa_s":
                            if tile == 0:
                                v = [x[:, held["v"], KEEP:2 * KEEP] for x in (WH, WL)]
                            else:
                                v = [x[0:rows, 8 * 128:9 * 128] for x in (VH, VL)]
                        else:
                            c = MEM + tile * 128
                            v = [x[:, held["v"], c:c + 128] for x in (WH, WL)]
                            n, q0 = DEC, 64
                        p = [x[0:rows, slot, j * 128 + q0:j * 128 + q0 + n] for x in (PTH, PTL)]
                        for a, b, k in ((0, 0, 0), (0, 1, 1), (1, 0, 2)):
                            mm(pe, PS[:, out:out + n], v[a], p[b], start=(first and k == 0), stop=(last and k == 2))
                        tile += 1
                    if gi == len(st["groups"]) - 1:
                        signal(o_full, now=True)
                    signal(pt_used)
                    if held_slot is not None:
                        signal(w_used)
                if st["kind"] in ("swa_s", "mem_s"):
                    signal(w_used)

            def attention(pe, steps, hooks, ready=None):
                if ready:
                    pe.wait_ge(*ready)
                elif steps[0]["kind"] != "mem_s":
                    pe.wait_ge(attn_ready, place.at("attn", 1))
                    place.add("attn")
                held_groups.clear()
                rings = [0]
                for st in steps:
                    rings.append(rings[-1] + len(st["groups"]))
                held = {}
                for s in range(-1, len(steps) + 3):
                    if 2 <= s < len(steps) + 2:
                        transposes(pe, steps[s - 2], s - 2)
                    early = s + 1 < len(steps) and s not in hooks and steps[0]["kind"] != "fox_s"
                    if early:
                        scores(pe, steps[s + 1], held)
                    if s >= 3:
                        values(pe, steps[s - 3], s - 3, rings[s - 3], held)
                    if s in hooks:
                        hooks[s]()
                    if s + 1 < len(steps) and not early:
                        scores(pe, steps[s + 1], held)
                place.add("step", len(steps))
                place.add("ring", rings[-1])

            def own_values(tile):
                return 128 if tile < NB else DEC

            pe0.wait_ge(memset_ok, 4)
            stat(pe0, MEM)

            def layer(pe, l):
                stat(pe, T)
                project(pe, HH, HL, CH, fresh=0)
                place.add("ntile", KT)

                def fox(pe, turn):
                    def one():
                        project(pe, HH, HL, CH)

                    one()
                    one()
                    n = len(fox_steps())
                    attention(pe, fox_steps(), {1: one, 2: lambda: value_hook(pe, 2), n - 1: one, n: one})
                    attention(pe, fox_steps(), {1: one, 2: lambda: value_hook(pe, 2)})
                    pe.wait_ge(o_free, place.at("step", 1))
                    down(pe, 0)

                repeat(pe, place, 2, fox)
                project(pe, HH, HL, CH)
                project(pe, HH, HL, CH)
                project(pe, HH, HL, CH)
                for pair in range(PAIRS):
                    hooks = {3: lambda: project(pe, HH, HL, CH)} if pair < PAIRS - 1 else {}
                    if pair == 0:
                        hooks[2] = lambda: value_hook(pe, 4)
                    attention(pe, swa_steps(pair), hooks)
                    if pair % 2:
                        pe.wait_ge(o_free, place.at("step", 1))
                        down(pe, 0)
                for m in range(2 * MEM_H):
                    project(pe, MH, ML, [(0, MEM)], fresh=0)
                    if m == STAT_AT - 1:
                        stat(pe, T)
                    if m > MEM_H:
                        value_tiles(pe, [[0, 1]], lambda tile: 128, 2)
                value_tiles(pe, [[0, 1]], lambda tile: 128, 1)
                place.add("ntile", KT)

                ready = (free[place.bank_set()], place.set_count(2))
                project(pe, HH, HL, CH, fresh=0)
                for head in range(MEM_H):
                    attention(pe, mem_steps(head), {3: lambda: project(pe, HH, HL, CH)} if head < MEM_H - 1 else {},
                              ready if head == 0 else None)
                    if head % 2:
                        pe.wait_ge(o_free, place.at("step", 1))
                        down(pe, 0)
                place.add("ntile", KT)
                stat(pe, T)

                def up(pe):
                    for _ in range(4):
                        project(pe, HH, HL, CH, fresh=0)

                def mix_down(pe, b):
                    pe.wait_ge(glu_ready, place.at("glu", 2))
                    down(pe, b)
                    place.add("glu", 2)

                up(pe)

                def mixer(pe, turn):
                    for b in range(2):
                        up(pe)
                        mix_down(pe, b)

                repeat(pe, place, (FT // 2 - 1) // 2, mixer)
                mix_down(pe, 0)
                place.add("ntile", KT)
                place.add("slab", 2)
                assert owed == [w_used]
                owed.clear()
                pe.drain().then_inc(w_used, 3)
                place.add("layer")

            repeat(pe0, place, DEPTH, layer)
            stat(pe0, T)

        def wait_all_read(eng, place):
            eng.wait_ge(free[0], place.uses_of(0, 1))
            eng.wait_ge(free[1], place.uses_of(1, 1))

        def wait_read(eng, place):
            eng.wait_ge(free[place.bank_set()], place.set_count(2))

        def wait_full(eng, place):
            eng.wait_ge(full[place.bank_set()], place.set_count(1))

        def step_areas(st):
            if st["heads"] == 1:
                return [(0, st["width"])]
            return [(p, p + n) for _, _, p, n, _, _, _ in st["pieces"]]

        @block.scalar
        def _(act0):
            place = Place()
            act0.sem_inc(t32_out, 16)
            act0.sem_inc(co_out, 16)

            def copy(act, out, in_):
                return act.activation(out, in_, ACT.Copy)

            def wait_own(act, ins):
                ins.then_inc(act_self, 1)
                place.add("self")
                act.wait_ge(act_self, place.at("self"))

            def hi(act, pieces):
                for out, in_ in pieces:
                    ins = copy(act, out, in_)
                ins.then_inc(hi_done, 1)

            def hi_tile(act, out):
                over_tile(place, lambda src, a, b: copy(act, like(out, a, b), src).then_inc(hi_done, 1))

            def fill_t32(act, width=T, last_reader=False):
                act.wait_ge(t32_out, place.at("store", 16, 16))
                if width == T:
                    ins = over_tile(place, lambda src, a, b: copy(act, like(T32, a, b), src), last_reader)
                else:
                    o = place.bank_set() * 1024
                    ins = copy(act, T32[:, 0:width], PS[:, o:o + width])
                return ins

            def store_t32(act, out, a, b):
                act.dma_start(out, T32[:, a:b]).then_inc(t32_out, 16)
                place.add("store")

            def group_hi(act, tiles_areas, out):
                act.wait_ge(g_full, place.at("group", 1))
                b = (6 + place.n["group"] % 2) * 512
                hi(act, [(out[0:rows, c:c + n], PS[0:rows, b + c:b + c + n]) for rows, c, n in tiles_areas])
                place.add("group")

            def value_groups(act, groups, rows_of, first=0):
                for tiles in groups:
                    areas = group_areas([(0, rows_of(t)) for t in tiles])
                    group_hi(act, areas, VH[:, (first + tiles[0]) * 128:])

            def squares(act, m, ready):
                ready()
                if m >= 3:
                    act.wait_ge(sq_used, place.at("norm", m - 2, 7))
                return ACC if m == 0 else SQ[m % 2]

            def split_sums(act, width):
                act.wait_ge(sq_used, place.at("norm", 7, 7))
                hi(act, [(SH[:, 0:width], ACC[:, 0:width])])

            def inverse_rms(act, out, width):
                wait_full(act, place)
                if width == T:
                    over_tile(place, lambda src, a, b: act.activation(like(out, a, b), src, ACT.Ln, bias=eps[:]),
                              last_reader=True)
                else:
                    o = place.bank_set() * 1024
                    act.activation(out[:, 0:width], PS[:, o:o + width], ACT.Ln, bias=eps[:])\
                        .then_inc(free[place.bank_set()], 1)
                wait_read(act, place)
                act.activation(out[:, 0:width], out[:, 0:width], ACT.Exp, scale=-0.5).then_inc(rms_ready, 1)
                place.add("use")
                place.add("norm")

            def tile_hi(act, dst, tmp, kt):
                act.wait_ge(ht_ready, place.at("ntile", kt + 1))
                hi(act, [(dst[:, kt, :], tmp(kt))])

            def normalised_hi(act, dst, tmp):
                for kt in range(KT):
                    tile_hi(act, dst, tmp, kt)
                place.add("ntile", KT)

            def attention(act, steps, r, hooks, each=None):
                n = len(steps)
                for s in range(n + 3):
                    if 2 <= s < n + 2:
                        for tiles in steps[s - 2]["groups"]:
                            act.wait_ge(pt_used, place.at("ring", 1))
                            slot = ring[0] % 3
                            group_hi(act, group_areas(tiles), PTH[:, slot, :])
                            ring[0] += 1
                            place.add("ring")
                    if s < n:
                        st = steps[s]
                        wait_read(act, place)
                        place.add("use")
                        if st["kind"] == "fox_s":
                            act.wait_ge(g_free, place.at("group", 3))
                            place.add("group")
                        for h, (a, b) in enumerate(step_areas(st)):
                            sink = st["pieces"][h][6]
                            if sink is not None:
                                act.activation(ES[:, s % 3, h:h + 1], NSK[:, sink:sink + 1], ACT.Exp,
                                               bias=NM[:, s % 3, h:h + 1], scale=-1.0)
                            p = probs(st, s % 3, a, b)
                            ins = act.activation(p, p, ACT.Exp,
                                                 bias=NM[:, s % 3, h:h + 1], scale=-1.0, accum_out=SM[:, s % 3, h:h + 1])
                        ins.then_inc(e_ready, 1)
                    if s >= 3:
                        act.wait_ge(o_full, place.at("step", s - 2))
                        hi(act, [(G0H[g:g + rows, r, t:t + m], PS[p:p + rows, OUTS + c:OUTS + c + m])
                                 for p, rows, c, g, t, m in steps[s - 3]["outs"]])
                    if each and 2 <= s < 2 + KT:
                        each(s - 2)
                    if s in hooks:
                        hooks[s]()
                place.add("step", n)
                ring[0] = 0

            ring = [0]

            def down(act, with_squares):
                for m in range(KT):
                    if with_squares:
                        dst = squares(act, m, lambda: wait_read(act, place))
                        act.activation(dst[:], XT[:, m, :], ACT.Square).then_inc(sq_ready, 1)
                    place.add("use")
                if with_squares:
                    split_sums(act, T)

            def rope_fill(act, base):
                if base is T32:
                    act.wait_ge(t32_out, place.at("store", 16, 16))
                wait_full(act, place)
                over_tile(place, lambda src, a, b: copy(act, like(base, a, b), src), last_reader=True)
                wait_read(act, place)
                place.add("use")
                place.add("rope")

            def rope_swap(act, base, quarters=range(4)):
                for g in quarters:
                    p, w = 32 * g, 32 * (g ^ 1)
                    act.dma_start(RX[p:p + 32, :], base[w:w + 32, :]).then_inc(swap_in, 16)

            act0.wait_ge(memset_ok, 4)
            act0.wait_ge(mem_in, 16)
            for m in range(KT):
                dst = squares(act0, m, lambda: None)
                act0.activation(dst[:, 0:MEM], MR[:, m, :], ACT.Square).then_inc(sq_ready, 1)
            split_sums(act0, MEM)
            inverse_rms(act0, RM, MEM)
            for m in range(KT):
                dst = squares(act0, m, lambda: act0.wait_ge(x_in[m], 16))
                act0.activation(dst[:], XT[:, m, :], ACT.Square).then_inc(sq_ready, 1)
            split_sums(act0, T)

            def layer(act, l):
                wait_all_read(act, place)
                act.dma_start(LC[:], layer_c[ds(l, 1)].rearrange("o p n -> p (o n)")).then_inc(lc_in, 16)
                act.dma_start(CLF[:], clogf[ds(l, 1)].rearrange("o p n -> p (o n)")).then_inc(lc_in, 16)
                inverse_rms(act, PR[:, 0, :], T)
                normalised_hi(act, HH, lambda kt: PR[:, 1 + kt % 2, :])

                act.wait_ge(lc_in, place.at("layer", 32, 32))
                wait_full(act, place)
                over_tile(place, lambda src, a, b: act.activation(like(FZ, a, b), src[0:8], ACT.Identity,
                                                                  bias=LC[0:8, C_BF:C_BF + 1]), last_reader=True)
                wait_read(act, place)
                place.add("use")
                wait_own(act, act.activation(FA[:], FZ[:], ACT.Abs))
                wait_own(act, act.activation(FA[:], FA[:], ACT.Exp, scale=-1.0))
                act.activation(FA[:], FA[:], ACT.Ln, bias=one[0:8, :]).then_inc(ln_done, 1)
                act.wait_ge(lf_ready, place.at("layer", 1))
                act.dma_start(o_lf[ds(l, 1)].rearrange("o p n -> p (o n)"), FL[:]).then_inc(lf_out, 16)
                act.wait_ge(c_ready, place.at("layer", 1))
                act.dma_start(decays, C8[:]).then_inc(c_stored, 16)

                def fox(act, turn):
                    def biases(pair):
                        wait_all_read(act, place)
                        act.wait_ge(c_stored, place.at("layer", 16, 16))
                        act.wait_ge(lf_out, place.at("layer", 16, 16))
                        for h in range(2):
                            row = decays[ds(pair * 2 + h, 1), :]
                            act.dma_start(XR[:, h, 0:SEQ], row[:, 0:SEQ].to_broadcast([128, SEQ])).then_inc(bias_in, 16)
                            act.dma_start(XR[64 * h:64 * h + 64, 2, :], row[:, SEQ:N_C8].to_broadcast([64, T])).then_inc(bias_in, 16)

                    def keys(pair):
                        wait_full(act, place)
                        fill_t32(act).then_inc(act_self, 1)
                        place.add("self")
                        hi_tile(act, KH)
                        act.wait_ge(act_self, place.at("self"))
                        store_t32(act, o_fk[ds(l * PAIRS + pair, 1)].rearrange("o p n -> p (o n)"), 0, T)
                        place.add("use")

                    def queries():
                        wait_full(act, place)
                        hi_tile(act, QH)
                        place.add("use")

                    def value_tile(pair):
                        wait_full(act, place)
                        fill_t32(act, last_reader=True)
                        wait_read(act, place)
                        place.add("use")
                        store_t32(act, o_fv[ds(l * PAIRS + pair, 1)].rearrange("o p n -> p (o n)"), 0, T)

                    def value_hook():
                        value_groups(act, V_GROUPS, lambda t: 128 if t < NB else DEC)

                    def next_keys():
                        biases(turn * 2 + 1)
                        keys(turn * 2 + 1)

                    keys(turn * 2)
                    queries()
                    biases(turn * 2)
                    n = len(fox_steps())
                    attention(act, fox_steps(), 0, {1: lambda: value_tile(turn * 2), 2: value_hook,
                                                    n - 1: next_keys, n: queries})
                    attention(act, fox_steps(), 1, {1: lambda: value_tile(turn * 2 + 1), 2: value_hook})
                    down(act, False)

                repeat(act, place, 2, fox)

                wait_all_read(act, place)
                act.dma_start(XR[:, 0, :], cos_t).then_inc(trig_in, 16)
                act.dma_start(XR[:, 1, :], sin_t).then_inc(trig_in, 16)
                rope_fill(act, T32)
                rope_swap(act, T32)
                act.wait_ge(roped, place.at("rope"))
                act.dma_start(o_sk[ds(l, 1)].rearrange("o p n -> p (o n)"), XR[:, 2, SEQ - KEEP:T]).then_inc(k32_out, 16)

                def window_values():
                    wait_full(act, place)
                    fill_t32(act, last_reader=True)
                    wait_read(act, place)
                    place.add("use")
                    store_t32(act, o_sv[ds(l, 1)].rearrange("o p n -> p (o n)"), SEQ - KEEP, T)

                def query_parts(pair):
                    if pair % 2 == 0:
                        act.wait_ge(t32_out, place.at("store", 16, 16))
                        act.wait_ge(roped, place.at("rope"))
                        g = 64 * (pair // 2)
                        copy(act, T32[0:64, :], XR[g:g + 64, 2, :])
                        wait_own(act, copy(act, T32[64:128, :], XR[g:g + 64, 2, :]))
                        hi(act, [(KH[:], T32[:])])
                    if pair == 0:
                        rope_fill(act, QX)
                        rope_swap(act, QX)
                    act.wait_ge(roped, place.at("rope"))
                    hi(act, [(QH[:], RX[:])])
                    if pair == PAIRS - 1:
                        act.wait_ge(k32_out, place.at("layer", 16, 16))
                        act.dma_start(MR[:, :, :], memT).then_inc(mem_in, 16)

                query_parts(0)
                window_values()
                for pair in range(PAIRS):
                    last = pair == PAIRS - 1
                    hooks = {} if last else {3: lambda: rope_fill(act, T32), 4: lambda: rope_swap(act, T32, (0, 1)),
                                             5: lambda: rope_swap(act, T32, (2, 3)), NB: lambda: query_parts(pair + 1)}
                    if pair == 0:
                        hooks[2] = lambda: value_groups(act, V_GROUPS, lambda t: 128 if t < NB else DEC)
                    attention(act, swa_steps(pair), pair % 2, hooks,
                              each=(lambda kt: tile_hi(act, MH, lambda kt: MT[:, kt % 2, :], kt)) if last else None)
                    if last:
                        place.add("ntile", KT)
                    if pair % 2:
                        down(act, last)

                def norm_tile(kt):
                    tile_hi(act, HH, lambda kt: PR[:, 1 + kt % 2, :], kt)

                for m in range(2 * MEM_H):
                    wait_full(act, place)
                    ins = fill_t32(act, MEM)
                    o = place.bank_set() * 1024
                    h = m % MEM_H
                    out = (o_mk if m < MEM_H else o_mv)[ds(l * MEM_H + h, 1)].rearrange("o p n -> p (o n)")
                    if m < MEM_H:
                        ins.then_inc(act_self, 1)
                        place.add("self")
                        hi(act, [(KH[:, h * MEM:(h + 1) * MEM], PS[:, o:o + MEM])])
                        act.wait_ge(act_self, place.at("self"))
                    else:
                        ins.then_inc(free[place.bank_set()], 1)
                        wait_read(act, place)
                    place.add("use")
                    store_t32(act, out, 0, MEM)
                    if m >= MEM_H:
                        value_groups(act, [[0, 1]], lambda t: 128, first=2 * h)
                    if m == STAT_AT - 1:
                        inverse_rms(act, PR[:, 0, :], T)
                    if m >= STAT_AT:
                        norm_tile(m - STAT_AT)
                for kt in range(2 * MEM_H - STAT_AT, KT):
                    norm_tile(kt)
                place.add("ntile", KT)

                def memory_queries(head):
                    wait_full(act, place)
                    hi_tile(act, QUERIES[head % 2][0])
                    place.add("use")

                memory_queries(0)
                for head in range(MEM_H):
                    attention(act, mem_steps(head), head % 2,
                              {3: lambda: memory_queries(head + 1)} if head < MEM_H - 1 else {})
                    if head % 2:
                        down(act, head == MEM_H - 1)
                inverse_rms(act, PR[:, 0, :], T)
                normalised_hi(act, HH, lambda kt: PR[:, 1 + kt % 2, :])

                act.wait_ge(co_out, place.at("layer", 16, 16))
                act.wait_ge(t32_out, place.at("store", 16, 16))

                def gates(act, f, g):
                    for r in range(2):
                        s = place.bank_set()
                        act.wait_ge(conv_done, place.at("glu", r + 1))
                        wait_full(act, place)
                        copy(act, CO[:, ds((f + r) * 4, 2)], PS[:, THIRD + SEQ - 770:THIRD + SEQ - 768])
                        copy(act, CO[:, ds((f + r) * 4 + 2, 2)], PS[:, THIRD + T - 770:THIRD + T - 768])
                        copy(act, GP[:, r, 770:2 + SEQ], PS[:, THIRD:THIRD + SEQ - 768])
                        copy(act, GP[:, r, SEQ + 4:T + 4], PS[:, THIRD + SEQ - 768:THIRD + T - 768]).then_inc(third_free, 1)
                        copy(act, GP[:, r, 2:770].rearrange("p (c n) -> p c n", c=2), parts(s)[1][0]).then_inc(free[s], 1)
                        copy(act, GP[:, r, SEQ + 2:SEQ + 4], LC[:, ds((f + r) * 2 + C_STATE, 2)]).then_inc(gate_ready, 1)
                        place.add("use")
                        act.wait_ge(conv_done, place.at("glu", r + 3))
                        act.activation(YY[:, r, 0:T + 2], YY[:, r, 0:T + 2], ACT.Silu).then_inc(silu_done, 1)
                        wait_read(act, place)
                        place.add("use")
                        hi(act, [(GH[g][:, r, 0:SEQ], YY[:, r, 0:SEQ]), (GH[g][:, r, SEQ:T], YY[:, r, SEQ + 2:T + 2])])
                    place.add("glu", 2)

                gates(act, 0, 0)

                def mixer(act, turn):
                    for b in range(2):
                        gates(act, turn * 4 + 2 * (b + 1), 1 - b)
                        down(act, False)

                repeat(act, place, (FT // 2 - 1) // 2, mixer)
                act.dma_start(o_cv[ds(l, 1)].rearrange("o p n -> p (o n)"), CO[:]).then_inc(co_out, 16)
                down(act, True)
                place.add("layer")

            repeat(act0, place, DEPTH, layer)
            inverse_rms(act0, PR[:, 0, :], T)
            for kt in range(KT):
                act0.wait_ge(y_ready, kt + 1)
                act0.dma_start(o_y[:, kt, :], YT[:, kt, :]).then_inc(out_done, 16)

        @block.vector
        def _(dve0):
            place = Place()
            dve0.sem_inc(free[0], 1)
            dve0.sem_inc(free[1], 1)
            dve0.sem_inc(third_free, 1)
            dve0.sem_inc(g_free, 2)
            dve0.sem_inc(o_free, 1)
            dve0.sem_inc(conv_done, 2)
            dve0.wait_ge(const_in, 80)
            dve0.tensor_copy(ident_r[:], ident[:]).then_inc(const_ok, 1)
            dve0.tensor_copy(causal_r[:], causal[:]).then_inc(const_ok, 1)
            dve0.tensor_copy(tail_mask_r[:], tail_mask[:]).then_inc(const_ok, 1)
            dve0.tensor_scalar(mean_r[:], ident[:], 0.0, 1.0 / D, ALU.mult, ALU.add).then_inc(const_ok, 1)
            dve0.memset(QSH[:].bitcast(F32), 0.0).then_inc(dve_self, 1)
            dve0.memset(QSL[:].bitcast(F32), 0.0).then_inc(const_ok, 1)
            dve0.wait_ge(memset_ok, 4)
            place.add("self")

            def wait_own(dve, ins):
                ins.then_inc(dve_self, 1)
                place.add("self")
                dve.wait_ge(dve_self, place.at("self"))

            def lo(dve, pieces):
                dve.wait_ge(hi_done, place.at("hi", 1))
                place.add("hi")
                for out, in_, high in pieces:
                    ins = dve.tensor_tensor(out, in_, high.bitcast(F32), ALU.subtract)
                return ins

            def lo_tile(dve, low, high):
                def part(src, a, b):
                    dve.wait_ge(hi_done, place.at("hi", 1))
                    place.add("hi")
                    return dve.tensor_tensor(like(low, a, b), src, like(high, a, b).bitcast(F32), ALU.subtract)

                over_tile(place, part, last_reader=True)
                place.add("use")

            def group_lo(dve, areas, low, high):
                b = (6 + place.n["group"] % 2) * 512
                lo(dve, [(low[0:rows, c:c + n], PS[0:rows, b + c:b + c + n], high[0:rows, c:c + n]) for rows, c, n in areas])\
                    .then_inc(g_free, 1)
                place.add("group")

            def value_groups(dve, groups, rows_of, first=0):
                for tiles in groups:
                    areas = group_areas([(0, rows_of(t)) for t in tiles])
                    c = (first + tiles[0]) * 128
                    group_lo(dve, areas, VL[:, c:], VH[:, c:])

            def sample_queries(dve):
                wait_all_read(dve, place)
                for out, src in ((QSH, QH), (QSL, QL)):
                    for h in range(2):
                        r = slice(64 * h, 64 * h + 64)
                        ins = dve.tensor_copy(out[r, r], src[r, SEQ:T].bitcast(F32))
                ins.then_inc(attn_ready, 1)
                place.add("attn")

            def add_square(dve, m, width=T):
                dve.wait_ge(sq_ready, place.at("norm", m + 1, 8))
                if m > 1:
                    dve.wait_ge(sq_used, place.at("norm", m - 1, 7))
                dve.tensor_tensor(ACC[:, 0:width], ACC[:, 0:width], SQ[m % 2][:, 0:width], ALU.add).then_inc(sq_used, 1)

            def split_sums(dve, width):
                lo(dve, [(SL[:, 0:width], ACC[:, 0:width], SH[:, 0:width])]).then_inc(stat_ready, 1)

            def await_rms(dve):
                place.add("use")
                place.add("norm")
                dve.wait_ge(rms_ready, place.at("norm"))

            def tile_scaled(dve, src, gains, scale, tmp, kt):
                if kt >= 2:
                    dve.wait_ge(h_ready, place.at("ntile", kt - 1))
                dve.scalar_tensor_tensor(tmp(kt), src(kt), gains[:, kt:kt + 1], scale, ALU.mult, ALU.mult)\
                    .then_inc(ht_ready, 1)

            def tile_lo(dve, tmp, high, low, kt):
                lo(dve, [(low[:, kt, :], tmp(kt), high[:, kt, :])]).then_inc(h_ready, 1)

            def normalised(dve, src, gains, scale, tmp, high, low):
                for kt in range(KT):
                    tile_scaled(dve, src, gains, scale, tmp, kt)
                    if kt >= 1:
                        tile_lo(dve, tmp, high, low, kt - 1)
                tile_lo(dve, tmp, high, low, KT - 1)
                place.add("ntile", KT)

            def attention(dve, steps, r, hooks, each=None, each_lo=None):
                n = len(steps)

                def norm(j):
                    st, k = steps[j], j % 3
                    dve.wait_ge(e_ready, place.at("step", j + 1))
                    h = st["heads"]
                    if st["pieces"][0][6] is not None:
                        wait_own(dve, dve.tensor_tensor(SM[:, k, 0:h], SM[:, k, 0:h], ES[:, k, 0:h], ALU.add))
                    wait_own(dve, dve.reciprocal(RC[:, k, 0:h], SM[:, k, 0:h]))
                    for i, (a, b) in enumerate(step_areas(st)):
                        p = probs(st, k, a, b)
                        ins = dve.tensor_scalar(p, p, RC[:, k, i:i + 1], None, ALU.mult)
                    ins.then_inc(p_ready, 1)

                for s in range(n + 3):
                    if s < n:
                        st = steps[s]
                        o = place.bank_set() * 1024
                        waits = [(full[place.bank_set()], place.set_count(1))]
                        if s == 0 and st["kind"] == "fox_s":
                            place.add("bias")
                            waits.append((bias_in, place.at("bias", 0, 64)))
                        if s >= 3:
                            waits.append((p_used, place.at("step", s + 1)))
                        wait_apart(dve, memset_ok, 4, waits)
                        heads = 0
                        for j, (where, c, p, m, bias, start, _) in enumerate(st["pieces"]):
                            if where == "set":
                                src, sig = PS[:, o + c:o + c + m], free[place.bank_set()]
                            else:
                                g = (6 + place.n["group"] % 2) * 512
                                wait_apart(dve, memset_ok, 4, [(g_full, place.at("group", 1)),
                                                               (free[place.bank_set()], place.set_count(2))])
                                src, sig = PS[:, g:g + m], g_free
                                place.add("group")
                            half_max = st["kind"] == "fox_s" and j == 0
                            acc = NM1[:] if half_max else NM[:, s % 3, heads:heads + 1]
                            ins = dve.tensor_tensor_reduce(probs(st, s % 3, p, p + m), src, bias, -st["scale"], start[:],
                                                           ALU.add, ALU.min, acc)
                            heads += not half_max
                            if half_max or j == len(st["pieces"]) - 1:
                                ins.then_inc(sig, 1)
                        place.add("use")
                    if 1 <= s < n + 1:
                        norm(s - 1)
                    if each and 3 <= s < 3 + KT:
                        each_lo(s - 3)
                    if 2 <= s < n + 2:
                        for tiles in steps[s - 2]["groups"]:
                            slot = ring[0] % 3
                            group_lo(dve, group_areas(tiles), PTL[:, slot, :], PTH[:, slot, :])
                            ring[0] += 1
                    if s >= 3:
                        lo(dve, [(G0L[g:g + rows, r, t:t + m], PS[p:p + rows, OUTS + c:OUTS + c + m], G0H[g:g + rows, r, t:t + m])
                                 for p, rows, c, g, t, m in steps[s - 3]["outs"]]).then_inc(o_free, 1)
                    if each and 2 <= s < 2 + KT:
                        each(s - 2)
                    if s in hooks:
                        hooks[s]()
                place.add("step", n)
                ring[0] = 0

            ring = [0]

            def down(dve, with_squares):
                wait_all_read(dve, place)
                for m in range(KT):
                    wait_full(dve, place)
                    over_tile(place, lambda src, a, b: dve.tensor_tensor(like(XT[:, m, :], a, b), src,
                                                                         like(XT[:, m, :], a, b), ALU.add), last_reader=True)
                    place.add("use")
                    if with_squares and m >= 2:
                        add_square(dve, m - 1)
                if with_squares:
                    add_square(dve, KT - 1)
                    split_sums(dve, T)

            def rope_product(dve, out, table):
                dve.wait_ge(trig_in, place.at("layer", 32, 32))
                dve.wait_ge(swap_in, place.at("rope", 64, 64))
                dve.tensor_tensor(out[:], out[:], XR[:, table, :], ALU.mult).then_inc(dve_self, 1)
                place.add("self")

            def rope_sum(dve, out, base):
                dve.wait_ge(dve_self, place.at("self"))
                dve.tensor_tensor(out, RX[:], base[:], ALU.add).then_inc(roped, 1)
                place.add("rope")

            def rotate(dve, out, base):
                place.add("use")
                rope_product(dve, base, 0)
                rope_product(dve, RX, 1)
                rope_sum(dve, out, base)

            for m in range(1, KT):
                add_square(dve0, m, MEM)
            split_sums(dve0, MEM)
            await_rms(dve0)
            for m in range(1, KT):
                add_square(dve0, m)
            split_sums(dve0, T)

            def layer(dve, l):
                await_rms(dve)
                dve.wait_ge(lc_in, place.at("layer", 32, 32))
                normalised(dve, lambda kt: XT[:, kt, :], LC[:, C_MIX:C_MIX + KT], PR[:, 0, :],
                           lambda kt: PR[:, 1 + kt % 2, :], HH, HL)
                dve.tensor_scalar(NSK[:], LC[:, C_SINK:C_STATE], -1.0, None, ALU.mult)

                dve.wait_ge(ln_done, place.at("layer", 1))
                place.add("use")
                dve.scalar_tensor_tensor(FL[:], FZ[:], 0.0, FA[:], ALU.min, ALU.subtract).then_inc(lf_ready, 1)
                dve.wait_ge(lf_ready, place.at("layer", 1))
                dve.wait_ge(h_ready, place.at("ntile"))
                dve.tensor_tensor_scan(C8[:, 0:SEQ], one[0:8, :].to_broadcast([8, SEQ]), FL[:, 0:SEQ], 0.0, ALU.mult, ALU.add)
                wait_own(dve, dve.tensor_tensor_scan(C8[:, SEQ:SEQ + PAST], one[0:8, :].to_broadcast([8, PAST]), CLF[:], 0.0,
                                                     ALU.mult, ALU.add))
                wait_own(dve, dve.tensor_tensor_scan(C8[:, SEQ + PAST:N_C8], one[0:8, :].to_broadcast([8, DEC]), FL[:, SEQ:T],
                                                     C8[:, SEQ + PAST - 1:SEQ + PAST], ALU.mult, ALU.add))
                dve.tensor_scalar(C8[:], C8[:], -1.0 / FOX_SCALE, None, ALU.mult).then_inc(c_ready, 1)

                def fox(dve, turn):
                    def keys():
                        lo_tile(dve, KL, KH)

                    def queries():
                        lo_tile(dve, QL, QH)
                        sample_queries(dve)

                    def skip_values():
                        place.add("use")

                    def value_hook():
                        value_groups(dve, V_GROUPS, lambda t: 128 if t < NB else DEC)

                    keys()
                    queries()
                    n = len(fox_steps())
                    attention(dve, fox_steps(), 0, {1: skip_values, 2: value_hook, n - 1: keys, n: queries})
                    attention(dve, fox_steps(), 1, {1: skip_values, 2: value_hook})
                    down(dve, False)

                repeat(dve, place, 2, fox)

                rotate(dve, XR[:, 2, :], T32)

                def query_parts(pair):
                    if pair % 2 == 0:
                        lo(dve, [(KL[:], T32[:], KH[:])])
                    if pair == 0:
                        place.add("use")
                        rope_product(dve, QX, 0)
                        rope_product(dve, RX, 1)
                        rope_sum(dve, RX[:], QX)
                    dve.wait_ge(roped, place.at("rope"))
                    wait_own(dve, lo(dve, [(QL[:], RX[:], QH[:])]))
                    sample_queries(dve)

                def rope_hooks():
                    return {3: lambda: place.add("use"), 5: lambda: rope_product(dve, T32, 0),
                            6: lambda: rope_product(dve, RX, 1), 7: lambda: rope_sum(dve, RX[:], T32)}

                def token_tile(kt):
                    if kt == 0:
                        dve.wait_ge(mem_in, place.at("layer", 32, 16))
                    tile_scaled(dve, lambda kt: MR[:, kt, :], LC[:, C_TOK:C_TOK + KT], RM[:], lambda kt: MT[:, kt % 2, :], kt)

                query_parts(0)
                place.add("use")
                for pair in range(PAIRS):
                    last = pair == PAIRS - 1
                    hooks = {} if last else rope_hooks() | {NB: lambda: query_parts(pair + 1)}
                    if pair == 0:
                        hooks[2] = lambda: value_groups(dve, V_GROUPS, lambda t: 128 if t < NB else DEC)
                    attention(dve, swa_steps(pair), pair % 2, hooks,
                              each=token_tile if last else None,
                              each_lo=lambda kt: tile_lo(dve, lambda kt: MT[:, kt % 2, :], MH, ML, kt))
                    if last:
                        place.add("ntile", KT)
                    if pair % 2:
                        down(dve, last)

                def norm_scaled(kt):
                    tile_scaled(dve, lambda kt: XT[:, kt, :], LC[:, C_MEM:C_MEM + KT], PR[:, 0, :],
                                lambda kt: PR[:, 1 + kt % 2, :], kt)

                def norm_lo(kt):
                    tile_lo(dve, lambda kt: PR[:, 1 + kt % 2, :], HH, HL, kt)

                for m in range(2 * MEM_H):
                    h = m % MEM_H
                    if m > STAT_AT:
                        norm_lo(m - STAT_AT - 1)
                    if m < MEM_H:
                        o = place.bank_set() * 1024
                        c = slice(h * MEM, (h + 1) * MEM)
                        lo(dve, [(KL[:, c], PS[:, o:o + MEM], KH[:, c])]).then_inc(free[place.bank_set()], 1)
                        place.add("use")
                    else:
                        place.add("use")
                        value_groups(dve, [[0, 1]], lambda t: 128, first=2 * h)
                    if m == STAT_AT - 1:
                        await_rms(dve)
                    if m >= STAT_AT:
                        norm_scaled(m - STAT_AT)
                for kt in range(2 * MEM_H - STAT_AT, KT):
                    norm_lo(kt - 1)
                    norm_scaled(kt)
                norm_lo(KT - 1)
                place.add("ntile", KT)

                def memory_queries(head):
                    lo_tile(dve, QUERIES[head % 2][1], QUERIES[head % 2][0])

                memory_queries(0)
                for head in range(MEM_H):
                    attention(dve, mem_steps(head), head % 2,
                              {3: lambda: memory_queries(head + 1)} if head < MEM_H - 1 else {})
                    if head % 2:
                        down(dve, head == MEM_H - 1)
                await_rms(dve)
                normalised(dve, lambda kt: XT[:, kt, :], LC[:, C_FFN:C_FFN + KT], PR[:, 0, :],
                           lambda kt: PR[:, 1 + kt % 2, :], HH, HL)
                for r in range(2):
                    ins = dve.memset(GP[:, r, 0:2], 0.0)
                wait_own(dve, ins)

                def gates(dve, f, g):
                    for r in range(2):
                        dve.wait_ge(gate_ready, place.at("glu", r + 1))
                        w = [LC[:, ds((f + r) * 3 + (C_CONV + j), 1)] for j in range(3)]
                        y = YY[:, r, 0:T + 2]
                        wait_own(dve, dve.tensor_scalar(y, GP[:, r, 0:T + 2], w[0], LC[:, ds((f + r) + C_BCONV, 1)],
                                                        ALU.mult, ALU.add))
                        wait_own(dve, dve.scalar_tensor_tensor(y, GP[:, r, 1:T + 3], w[1], y, ALU.mult, ALU.add))
                        dve.scalar_tensor_tensor(y, GP[:, r, 2:T + 4], w[2], y, ALU.mult, ALU.add).then_inc(conv_done, 1)
                        place.add("use")
                        s = place.bank_set()
                        wait_full(dve, place)
                        dve.wait_ge(silu_done, place.at("glu", r + 1))
                        y2 = YY[:, r, 0:768].rearrange("p (c n) -> p c n", c=2)
                        y3, y4 = YY[:, r, 768:SEQ], YY[:, r, SEQ + 2:T + 2]
                        dve.tensor_tensor(y3, PS[:, THIRD:THIRD + SEQ - 768], y3, ALU.mult)
                        dve.tensor_tensor(y4, PS[:, THIRD + SEQ - 768:THIRD + T - 768], y4, ALU.mult).then_inc(third_free, 1)
                        dve.tensor_tensor(y2, parts(s)[1][0], y2, ALU.mult).then_inc(free[s], 1)
                        place.add("use")
                        lo(dve, [(GL[g][:, r, 0:SEQ], YY[:, r, 0:SEQ], GH[g][:, r, 0:SEQ]),
                                 (GL[g][:, r, SEQ:T], YY[:, r, SEQ + 2:T + 2], GH[g][:, r, SEQ:T])]).then_inc(glu_ready, 1)
                    place.add("glu", 2)

                gates(dve, 0, 0)

                def mixer(dve, turn):
                    for b in range(2):
                        gates(dve, turn * 4 + 2 * (b + 1), 1 - b)
                        down(dve, False)

                repeat(dve, place, (FT // 2 - 1) // 2, mixer)
                down(dve, True)
                place.add("layer")

            repeat(dve0, place, DEPTH, layer)
            await_rms(dve0)
            for kt in range(KT):
                dve0.scalar_tensor_tensor(YT[:, kt, :], XT[:, kt, :], FC[:, kt:kt + 1], PR[:, 0, :], ALU.mult, ALU.mult)\
                    .then_inc(y_ready, 1)


def _in_blocks(w):
    return w.reshape(2, 4, 128, 128).transpose(0, 2, 1, 3).reshape(2, 128, HALF)


def _out_blocks(w2):
    return w2.reshape(2, 128, 2, HALF).transpose(2, 0, 1, 3).reshape(4, 128, HALF)


def _layer_slabs(x, l):
    w_in = x["w_in"][l]
    fox = FOX_H * HD
    f0, s0 = 3 * fox, 3 * fox + FOX_H
    k0, v0 = s0 + SWA_H * HD, s0 + SWA_H * HD + SWA_KV * HD
    out = [_in_blocks(np.tile(w_in[:, f0:s0], (1, 16)))]
    w_out = x["w_out"][l].reshape(8, 128, D)
    ck, cv = x["cache_fox_k"][l, 0], x["cache_fox_v"][l, 0]

    def fox_part(a, p):
        return _in_blocks(w_in[:, a * fox + p * 128:a * fox + (p + 1) * 128])

    for p in range(PAIRS):
        if p % 2 == 0:
            out += [fox_part(1, p), fox_part(0, p)]
        kp = ck[:, 2 * p:2 * p + 2].reshape(PAST, 128)
        vp = cv[:, 2 * p:2 * p + 2].reshape(PAST, 128)
        out.append(kp.T.reshape(128, 2, HALF).transpose(1, 0, 2))
        out.append(fox_part(2, p))
        out.append(vp.reshape(2, 4, 128, 128).transpose(0, 2, 1, 3).reshape(2, 128, HALF))
        out += [fox_part(1, p + 1), fox_part(0, p + 1)] if p % 2 == 0 else [_out_blocks(w_out[p - 1:p + 1])]
    out.append(_in_blocks(w_in[:, k0:v0]))
    sk, sv = x["cache_swa_k"][l, 0], x["cache_swa_v"][l, 0]

    def window_queries(p):
        return [_in_blocks(w_in[:, s0 + p * 128:s0 + (p + 1) * 128])] if p < PAIRS else []

    out += window_queries(0)
    out.append(_in_blocks(w_in[:, v0:v0 + 128]))
    for p in range(PAIRS):
        kt = sk[:, p // 2].T
        out.append(np.concatenate([np.concatenate([kt, kt]), sv.reshape(KEEP, 128), np.zeros((128, 256), np.float32)], 1)[None])
        out += window_queries(p + 1)
        if p % 2:
            out.append(_out_blocks(w_out[PAIRS + p - 1:PAIRS + p + 1]))
    for w in (x["w_mk"][l], x["w_mv"][l]):
        for m in range(MEM_H):
            out.append(_in_blocks(w[:, m * 128:(m + 1) * 128]))
    w_mo = x["w_mo"][l].reshape(MEM_H, 128, D)

    def memory_queries(m):
        return [_in_blocks(x["w_mq"][l][:, m * 128:(m + 1) * 128])] if m < MEM_H else []

    out += memory_queries(0)
    for m in range(MEM_H):
        mk, mv = x["cache_mem_k"][l, 0, :, m], x["cache_mem_v"][l, 0, :, m]
        out.append(np.concatenate([mk.T, mv.reshape(2, 128, 128).transpose(1, 0, 2).reshape(128, 256)], 1)[None])
        out += memory_queries(m + 1)
        if m % 2:
            out.append(_out_blocks(w_mo[m - 1:m + 1]))
    w_up, w_down = x["w_up"][l], x["w_down"][l].reshape(FT, 128, D)

    def up(g):
        for f in (2 * g, 2 * g + 1):
            out.append(_in_blocks(w_up[:, f * 128:(f + 1) * 128]))
            out.append(_in_blocks(w_up[:, FF + f * 128:FF + (f + 1) * 128]))

    up(0)
    for g in range(1, FT // 2):
        up(g)
        out.append(_out_blocks(w_down[2 * g - 2:2 * g]))
    out.append(_out_blocks(w_down[FT - 2:FT]))
    out.append(np.zeros((2, 128, HALF), np.float32))
    out = np.concatenate(out)
    assert out.shape == (N_SLABS, 128, HALF), out.shape
    return out


def _layer_constants(x, l):
    def columns(v):
        return v.reshape(-1, 128).T

    c = [columns(x[n][l]) for n in ("ln_mix", "ln_mem", "ln_memtok", "ln_ffn")]
    c.append(x["w_conv"][l].reshape(3, FT, 128).transpose(2, 1, 0).reshape(128, 3 * FT))
    c.append(columns(x["b_conv"][l]))
    c.append(np.tile(x["b_f"][l], 16)[:, None])
    sinks = x["swa_sinks"][l]
    c.append(np.broadcast_to(sinks, (128, SWA_H)))
    c.append(np.repeat(sinks.reshape(PAIRS, 2).T, 64, axis=0))
    c.append(x["state_conv"][l, 0].reshape(2, FT, 128).transpose(2, 1, 0).reshape(128, 2 * FT))
    return np.concatenate(c, 1)


_OUTS = [("y", (128, KT, T)), ("fk", (DEPTH * PAIRS, 128, T)), ("fv", (DEPTH * PAIRS, 128, T)),
         ("lf", (DEPTH, 8, T)), ("sk", (DEPTH, 128, KEEP + DEC)), ("sv", (DEPTH, 128, KEEP + DEC)),
         ("mk", (DEPTH * MEM_H, 128, MEM)), ("mv", (DEPTH * MEM_H, 128, MEM)), ("cv", (DEPTH, 128, FT * 4)),
         ("tk", (DEPTH, KEEP - DEC, 128)), ("tv", (DEPTH, KEEP - DEC, 128))]


def kernel(**inputs):
    import concourse.bacc as _bacc
    from concourse import mybir as _mybir
    from concourse.bass_utils import run_bass_kernel_spmd as _run

    x = {n: np.asarray(v) for n, v in inputs.items()}
    tokens = np.concatenate([x["x_prompt"][0], x["x_sample"][0]])

    def feature_major(v):
        return v.T.reshape(KT, 128, -1).transpose(1, 0, 2)

    data = {
        "xT": feature_major(tokens),
        "memT": feature_major(x["mem_prompt"][0]),
        "slabs": np.concatenate([_layer_slabs(x, l) for l in range(DEPTH)]),
        "layer_c": np.stack([_layer_constants(x, l) for l in range(DEPTH)]),
        "final_c": x["ln_final"].reshape(KT, 128).T,
        "clogf": x["cache_fox_logf"][:, 0].transpose(0, 2, 1),
        "swa_tail_k": x["cache_swa_k"][:, 0, DEC:].reshape(DEPTH, KEEP - DEC, 128),
        "swa_tail_v": x["cache_swa_v"][:, 0, DEC:].reshape(DEPTH, KEEP - DEC, 128),
    }
    nc = _bacc.Bacc("TRN2", target_bir_lowering=False, num_devices=1, dynamic_dma_scratch_size=1024)
    arrays, args = {}, []
    for name, a in data.items():
        a = np.ascontiguousarray(a)
        arrays[f"in_{name}"] = a
        args.append(nc.dram_tensor(f"in_{name}", a.shape, _mybir.dt.from_np(a.dtype), kind="ExternalInput").ap())
    for name, shape in _OUTS:
        args.append(nc.dram_tensor(f"out_{name}", shape, _mybir.dt.float32, kind="ExternalOutput").ap())
    encoder_step(nc, *args)
    r = _run(nc, [arrays], core_ids=[0]).results[0]
    got = {name: r[f"out_{name}"] for name, _ in _OUTS}

    def heads(a, n, hd, tokens):
        a = a.reshape(DEPTH, n * hd, -1).transpose(0, 2, 1)[:, tokens]
        return a.reshape(DEPTH, 1, a.shape[1], n, hd)

    prompt, sample = slice(0, SEQ), slice(SEQ, T)
    y = got["y"].transpose(2, 1, 0).reshape(T, D)
    lf = got["lf"].transpose(0, 2, 1)
    cv = got["cv"].reshape(DEPTH, 128, FT, 2, 2).transpose(3, 0, 4, 2, 1).reshape(2, DEPTH, 1, 2, FF)

    def window(tail, own):
        a = np.concatenate([tail, own.transpose(0, 2, 1)[:, KEEP:]], 1)
        return a.reshape(DEPTH, 1, KEEP, SWA_KV, HD)

    return (y[None, prompt], y[None, sample],
            heads(got["fk"], FOX_H, HD, prompt), heads(got["fv"], FOX_H, HD, prompt), lf[:, None, prompt],
            heads(got["sk"], SWA_KV, HD, slice(0, KEEP)), heads(got["sv"], SWA_KV, HD, slice(0, KEEP)),
            heads(got["mk"], MEM_H, 128, slice(0, MEM)), heads(got["mv"], MEM_H, 128, slice(0, MEM)), cv[0],
            heads(got["fk"], FOX_H, HD, sample), heads(got["fv"], FOX_H, HD, sample), lf[:, None, sample],
            window(got["tk"], got["sk"]), window(got["tv"], got["sv"]), cv[1])
```
